# Optimizing a Trainium2 kernel written in Bass

```python
import jax, jax.numpy as jnp
from jax import lax
import numpy as np

D_MODEL = 1024
BATCH = 1
SEQ = 1024
DEPTH = 1
DEC_BATCH = 1
DEC_SEQ = 256
PAST_LEN = 128

GRID_W = 64
N_HEADS_NA = 8
HEAD_DIM = 64
NA_WIDTH = N_HEADS_NA * HEAD_DIM
NA_KH = 8
NA_KW = 16
N_FOURIER_GROUPS = 4
FOURIER_GROUP_DIM = 128
FOURIER_WIDTH = N_FOURIER_GROUPS * FOURIER_GROUP_DIM
IN_WIDTH = 3 * NA_WIDTH + FOURIER_WIDTH + 2 * D_MODEL
SPLITS = (NA_WIDTH, 2 * NA_WIDTH, 3 * NA_WIDTH, 3 * NA_WIDTH + FOURIER_WIDTH,
          3 * NA_WIDTH + FOURIER_WIDTH + D_MODEL)
N_EXPERTS = 16
EXPERT_FF = 2048
EC_CAPACITY_FACTOR = 2
RMS_EPS = 1e-6

kernel_name = "hybrid_na_fnet_ec_encoder"

def rmsnorm(x, g):
    xf = x.astype(jnp.float32)
    y = xf * lax.rsqrt(jnp.mean(xf * xf, axis=-1, keepdims=True) + RMS_EPS)
    return (y * g.astype(jnp.float32)).astype(x.dtype)

def neighborhood_attention(q, k, v, rpb):
    B, S, H, Dh = q.shape
    rows = S // GRID_W
    kh = min(NA_KH, rows)
    kw = NA_KW
    r = jnp.arange(rows)
    c = jnp.arange(GRID_W)
    r0 = jnp.clip(r - kh // 2, 0, rows - kh)
    c0 = jnp.clip(c - kw // 2, 0, GRID_W - kw)
    key_r = r0[:, None] + jnp.arange(kh)
    key_c = c0[:, None] + jnp.arange(kw)
    key_idx = (key_r[:, None, :, None] * GRID_W
               + key_c[None, :, None, :]).reshape(rows, GRID_W, kh * kw)
    dr = key_r - r[:, None]
    dc = key_c - c[:, None]
    scale = HEAD_DIM ** -0.5
    qb = q.reshape(B, rows, GRID_W, H, Dh).transpose(1, 0, 2, 3, 4)

    def row_block(args):
        q_r, idx_r, dr_r = args
        k_r = k[:, idx_r]
        v_r = v[:, idx_r]
        bias = rpb[:, dr_r[None, :, None] + (NA_KH - 1),
                   dc[:, None, :] + (NA_KW - 1)]
        bias = bias.reshape(H, GRID_W, kh * kw).astype(jnp.float32)
        s = jnp.einsum('bqhd,bqnhd->bhqn', q_r, k_r).astype(jnp.float32) * scale + bias[None]
        p = jax.nn.softmax(s, axis=-1).astype(v.dtype)
        return jnp.einsum('bhqn,bqnhd->bqhd', p, v_r)

    out = lax.map(row_block, (qb, key_idx, dr))
    return out.transpose(1, 0, 2, 3, 4).reshape(B, S, H * Dh)

def fourier_mix(f):
    B, S, _ = f.shape
    u = f.reshape(B, S, N_FOURIER_GROUPS, FOURIER_GROUP_DIM).astype(jnp.float32)
    re = jnp.fft.fft2(u, axes=(1, 3), norm="ortho").real
    return re.reshape(B, S, FOURIER_WIDTH).astype(f.dtype)

def expert_choice_ffn(h, w_router, w_gate_e, w_up_e, w_down_e):
    N, D = h.shape
    cap = EC_CAPACITY_FACTOR * N // N_EXPERTS
    aff = jax.nn.softmax((h @ w_router).astype(jnp.float32), axis=-1)
    gates, idx = lax.top_k(aff.T, cap)
    xe = h[idx]

    def one_expert(args):
        xc, wg, wu, wd = args
        a = xc @ wg
        b = xc @ wu
        return (jax.nn.silu(a) * b) @ wd

    ye = lax.map(one_expert, (xe, w_gate_e, w_up_e, w_down_e))
    ye = ye * gates[..., None].astype(ye.dtype)
    return jnp.zeros_like(h).at[idx.reshape(-1)].add(ye.reshape(-1, D))

def encoder_layer(x, norm1_g, w_in, q_norm_g, k_norm_g, rpb, w_na_out, w_fourier,
                  w_out, norm2_g, w_router, w_gate_e, w_up_e, w_down_e):
    B, S, D = x.shape
    h = rmsnorm(x, norm1_g)
    z = h @ w_in
    q, k, v, f, ga, gf = jnp.split(z, SPLITS, axis=-1)
    q = rmsnorm(q.reshape(B, S, N_HEADS_NA, HEAD_DIM), q_norm_g)
    k = rmsnorm(k.reshape(B, S, N_HEADS_NA, HEAD_DIM), k_norm_g)
    v = v.reshape(B, S, N_HEADS_NA, HEAD_DIM)
    o_na = neighborhood_attention(q, k, v, rpb) @ w_na_out
    o_f = fourier_mix(f) @ w_fourier
    merged = jax.nn.sigmoid(ga) * o_na + jax.nn.sigmoid(gf) * o_f
    x = x + merged @ w_out
    h2 = rmsnorm(x, norm2_g).reshape(B * S, D)
    x = x + expert_choice_ffn(h2, w_router, w_gate_e, w_up_e, w_down_e).reshape(B, S, D)
    return x

def setup_inputs(seed: int = 0) -> dict:
    key = jax.random.key(seed)
    ks = jax.random.split(key, 16)
    f32 = jnp.float32
    nrm = lambda k, shape, s: jax.random.normal(k, shape, f32) * s
    return {
        "x_prompt": nrm(ks[0], (BATCH, SEQ, D_MODEL), 1.0),
        "x_sample": nrm(ks[1], (DEC_BATCH, DEC_SEQ, D_MODEL), 1.0),
        "norm1_g": 1.0 + nrm(ks[2], (DEPTH, D_MODEL), 0.02),
        "w_in": nrm(ks[3], (DEPTH, D_MODEL, IN_WIDTH), D_MODEL ** -0.5),
        "q_norm_g": 1.0 + nrm(ks[4], (DEPTH, HEAD_DIM), 0.02),
        "k_norm_g": 1.0 + nrm(ks[5], (DEPTH, HEAD_DIM), 0.02),
        "rpb": nrm(ks[6], (DEPTH, N_HEADS_NA, 2 * NA_KH - 1, 2 * NA_KW - 1), 0.5),
        "w_na_out": nrm(ks[7], (DEPTH, NA_WIDTH, D_MODEL), NA_WIDTH ** -0.5),
        "w_fourier": nrm(ks[8], (DEPTH, FOURIER_WIDTH, D_MODEL), FOURIER_WIDTH ** -0.5),
        "w_out": nrm(ks[9], (DEPTH, D_MODEL, D_MODEL), D_MODEL ** -0.5),
        "norm2_g": 1.0 + nrm(ks[10], (DEPTH, D_MODEL), 0.02),
        "w_router": nrm(ks[11], (DEPTH, D_MODEL, N_EXPERTS), D_MODEL ** -0.5),
        "w_gate_e": nrm(ks[12], (DEPTH, N_EXPERTS, D_MODEL, EXPERT_FF), D_MODEL ** -0.5),
        "w_up_e": nrm(ks[13], (DEPTH, N_EXPERTS, D_MODEL, EXPERT_FF), D_MODEL ** -0.5),
        "w_down_e": nrm(ks[14], (DEPTH, N_EXPERTS, EXPERT_FF, D_MODEL), EXPERT_FF ** -0.5),
    }

def reference(x_prompt, x_sample, norm1_g, w_in, q_norm_g, k_norm_g, rpb, w_na_out,
              w_fourier, w_out, norm2_g, w_router, w_gate_e, w_up_e, w_down_e):
    def trunk(x):
        for l in range(DEPTH):
            x = encoder_layer(x, norm1_g[l], w_in[l], q_norm_g[l], k_norm_g[l], rpb[l],
                              w_na_out[l], w_fourier[l], w_out[l], norm2_g[l],
                              w_router[l], w_gate_e[l], w_up_e[l], w_down_e[l])
        return x

    y_prompt = trunk(x_prompt)
    y_sample = trunk(x_sample)
    return (y_prompt, y_sample)


_drawn_inputs = setup_inputs


def setup_inputs(seed=0):
    import zlib

    import numpy as np

    out = dict(_drawn_inputs(seed))
    spreads = {}
    factors = {'norm1_g': 4.265, 'q_norm_g': 7.334, 'k_norm_g': 8.0, 'norm2_g': 3.862}
    for name, (base, spread) in spreads.items():
        noise = np.random.default_rng([zlib.crc32(name.encode()), seed]).standard_normal(out[name].shape)
        drawn = base * np.exp(spread * noise) if base else spread * noise
        out[name] = __import__('jax').numpy.asarray(drawn.astype(out[name].dtype))
    for name, factor in factors.items():
        out[name] = (out[name] * factor).astype(out[name].dtype)
    return out
```

```python
from contextlib import ExitStack

import concourse.bass as bass
import concourse.mybir as mybir
import numpy as np

F32 = mybir.dt.float32
F32R = mybir.dt.float32r
BF16 = mybir.dt.bfloat16
U32 = mybir.dt.uint32
ALU = mybir.AluOpType
ACT = mybir.ActivationFunctionType
AX = mybir.AxisListType

P = 128
D = 1024
KT = D // P
S_PROMPT, S_SAMPLE = 1024, 256
TOK = S_PROMPT + S_SAMPLE
NT = TOK // P
PT_TILES = S_PROMPT // P
CHUNKS = [(0, 512), (512, 512), (1024, 256)]
BANK = 512
GRID = 64
HEADS, DH = 8, 64
NA = HEADS * DH
KH, KW = 8, 16
FG, FD = 4, 128
F_COL = 3 * NA
GA_COL = F_COL + FG * FD
GF_COL = GA_COL + D
IN_W = GF_COL + D
EXPERTS, FF = 16, 2048
FT = FF // P
CAP_P = 2 * S_PROMPT // EXPERTS
CAP_S = 2 * S_SAMPLE // EXPERTS
CAP = CAP_P + CAP_S
EPS = 1e-6
MASKED = -1e30
BIAS_ROWS = 14
INNER_ROWS = KH + 1
RPB_H, RPB_W = 2 * KH - 1, 2 * KW - 1
BRANCH_BANKS = (6, 7, 0, 1, 2, 3)
P_SLOTS = 3
SKEW = 2 * GRID - 1


CHUNKS_E, UNITS = 12, 24
RAW_SLOTS, UNIT_SLOTS, LEAD = 4, 6, 4


def place_of(v):
    return (2 * (v // 4) + v % 2, v // 2 % 2) if v < 16 else (8 + (v - 16) // 2, v % 2)


def ahead(step):
    return [2 * step + LEAD, 2 * step + LEAD + 1] if step < 8 else [step + 8 + LEAD]


POOLS = [v for v in range(UNITS) if v % 3 == 2]
DVES = [v for v in range(UNITS) if v % 3 != 2]


def attention_tiles():
    tiles = []
    for base, rows in ((0, S_PROMPT // GRID), (S_PROMPT, S_SAMPLE // GRID)):
        kh = min(KH, rows)
        for r in range(0, rows, 2):
            lo = min(max(r - kh // 2, 0), rows - kh)
            hi = min(max(r + 1 - kh // 2, 0), rows - kh) + kh
            tiles.append((base + lo * GRID, hi - lo, lo - r + KH - 2, hi - lo > kh))
    return tiles


TILES = attention_tiles()
X_BANKS = ((6, 0, 3), (7, 3, 3), (0, 6, 2))
Y_BANKS = ((1, 2), (6, 7))


def build(nc, x, g1, w_in, q_g, k_g, rpb, w_na, w_fo, w_out, g2, w_r, w_g, w_u, w_d,
          dft_c, pos_c, pos_s, spos_c, spos_s, col_mask, y):
    ctx = ExitStack()
    with ctx:
        def sem(name):
            return ctx.enter_context(nc.semaphore(name))

        skew = nc.dram_tensor("skew_dram", (HEADS * RPB_H, GRID, SKEW), F32, kind="Internal").ap()
        xn_dram = nc.dram_tensor("xn_dram", (TOK, D), F32, kind="Internal").ap()

        base = -(-nc.sbuf_base // 32) * 32
        cursor = [base]

        def region(nbytes):
            at = cursor[0]
            cursor[0] += -(-nbytes // 32) * 32
            return at

        def at(name, shape, offset, dt=F32):
            return nc.alloc_sbuf_tensor_at(name, shape, dt, offset=offset)

        def put(name, shape, dt=F32):
            return at(name, shape, region(4 * int(np.prod(shape[1:]))), dt)

        ident = put("ident", [P, P])
        early_at = region(0)
        head_ones = put("head_ones", [P, P])
        mask_sb = put("mask_sb", [P, GRID])
        rpb_pad = put("rpb_pad", [HEADS * RPB_H, SKEW])
        assert region(0) - early_at >= 8 * CAP
        g1_sb = put("g1_sb", [P, KT])
        g2_sb = put("g2_sb", [P, KT])
        qk_g = put("qk_g", [P, 2])
        eps = put("eps", [P, 1])
        wr_sb = put("wr_sb", [P, KT, EXPERTS])
        ss = put("ss", [P, 2])
        lnv = put("lnv", [P, 2])
        rstd = put("rstd", [P, 2])
        row_max = put("row_max", [P, P_SLOTS])
        neg_max = put("neg_max", [P, P_SLOTS])
        row_sum = put("row_sum", [P, P_SLOTS])
        row_rec = put("row_rec", [P, P_SLOTS])
        gate_t = put("gate_t", [P, 2, EXPERTS + 1])
        idx_t = put("idx_t", [P, 2, EXPERTS + 1], U32)
        gate_now = put("gate_now", [P, 2])
        idx_gather = put("idx_gather", [P, 2], U32)
        idx_scatter = put("idx_scatter", [P, 2], U32)

        H0 = region(0)
        hT = put("hT", [P, KT, TOK])
        ofT = put("ofT", [P, FG, TOK])
        onaT = put("onaT", [P, NA // P, TOK])
        Z0 = cursor[0]
        Z = [Z0]

        def z(name, shape, dt=F32):
            t = at(name, shape, Z[0], dt)
            Z[0] += -(-(2 if dt == BF16 else 4) * int(np.prod(shape[1:])) // 32) * 32
            return t

        pos_c_sb = z("pos_c_sb", [P, PT_TILES, S_PROMPT])
        pos_s_sb = z("pos_s_sb", [P, PT_TILES, S_PROMPT])
        spos_c_sb = z("spos_c_sb", [P, NT - PT_TILES, S_SAMPLE])
        spos_s_sb = z("spos_s_sb", [P, NT - PT_TILES, S_SAMPLE])
        dft_sb = z("dft_sb", [P, 2 * FD])
        f_w = z("f_w", [P, KT, FD])
        fT = z("fT", [P, TOK])
        f_mix = z("f_mix", [P, NT, 2 * FD])
        h_w_at = Z[0]
        h_w = z("h_w", [P, 3, KT, P])
        bias_raw = z("bias_raw", [P, 2, BIAS_ROWS, GRID])
        assert Z[0] <= nc.sbuf_usable_end
        Z[0] = Z0
        x_in = [z(f"x_in{u}", [P, D]) for u in range(2)]
        xn_a = [z(f"xn_a{u}", [P, D]) for u in range(2)]
        junk_a = z("junk_a", [P, D])
        Z[0] = Z0
        qkvT = z("qkvT", [P, 3, TOK])
        v_tok = z("v_tok", [P, NT, P])
        bias_all = z("bias_all", [P, 2, BIAS_ROWS, GRID])
        bias_in = z("bias_in", [P, 2, INNER_ROWS, GRID])
        p_sb = [z(f"p_sb{u}", [P, INNER_ROWS * GRID]) for u in range(P_SLOTS)]
        pT = [z(f"pT{u}", [P, 5, P]) for u in range(2)]
        sq = [z(f"sq{u}", [P, BANK]) for u in range(2)]
        rinv = [z(f"rinv{u}", [P, BANK]) for u in range(2)]
        hx_at = Z[0]
        hx_hi = [z(f"hx_hi{c}", [P, KT, cn], F32R) for c, (_, cn) in enumerate(CHUNKS[:2])]
        gated = [z(f"gated{u}", [P, BANK]) for u in range(2)]
        assert Z[0] <= h_w_at
        Z[0] = h_w_at
        hx_hi.append(z("hx_hi2", [P, KT, CHUNKS[2][1]], F32R))
        hx_lo = at("hx_lo", [P, KT, TOK], H0, F32R)
        m_raw = [z(f"m_raw{u}", [P, KT, P]) for u in range(2)]
        m_hi = [z(f"m_hi{u}", [P, KT, P], F32R) for u in range(2)]
        m_lo = [z(f"m_lo{u}", [P, KT, P], F32R) for u in range(2)]
        m_w = [z(f"m_w{u}", [P, 4, P]) for u in range(2)]
        assert Z[0] <= nc.sbuf_usable_end
        Z[0] = Z0
        mT = z("mT", [P, KT, TOK])
        sig_at = Z[0]
        sig = [z(f"sig{u}", [P, TOK]) for u in range(2)]
        assert Z[0] <= hx_at
        Z[0] = sig_at
        w_out_sb = z("w_out_sb", [P, KT, D])
        Z[0] = Z0 + 4 * (KT * TOK + KT * D)
        x_res = [z(f"x_res{u}", [P, D]) for u in range(2)]
        x1 = [z(f"x1_{u}", [P, D]) for u in range(2)]
        xn = [z(f"xn{u}", [P, D]) for u in range(2)]
        h2T = [z(f"h2T{u}", [P, KT, P]) for u in range(2)]
        r_at = Z[0]
        m_tok = [z(f"m_tok{u}", [P, KT, P]) for u in range(2)]
        junk_o = z("junk_o", [P, D])
        log_at = Z[0]
        logT = z("logT", [EXPERTS, TOK])
        assert Z[0] <= nc.sbuf_usable_end
        Z[0] = r_at
        log_tok = z("log_tok", [P, NT, EXPERTS])
        aff_tok = z("aff_tok", [P, NT, EXPERTS])
        r_max = z("r_max", [P, NT])
        r_sum = z("r_sum", [P, NT])
        aff = z("aff", [EXPERTS, TOK])
        top_v = z("top_v", [EXPERTS, CAP])
        top_i = z("top_i", [EXPERTS, CAP], U32)
        top_f = z("top_f", [EXPERTS, CAP])
        assert Z[0] <= log_at
        Z[0] = H0
        raw = [z(f"raw{s}", [P, KT * 512]) for s in range(RAW_SLOTS)]
        xg_p = z("xg_p", [P, D])
        xg_s = z("xg_s", [CAP_S, D])
        ye_p = z("ye_p", [P, D])
        ye_s = z("ye_s", [CAP_S, D])
        assert Z[0] <= Z0
        w_hi = [z(f"w_hi{s}", [P, KT * 256], F32R) for s in range(UNIT_SLOTS)]
        w_lo = [z(f"w_lo{s}", [P, KT * 256], BF16) for s in range(UNIT_SLOTS)]
        assert Z[0] <= Z0 + 4 * (KT * TOK + KT * D)
        act_hl = z("act_hl", [P, FT, 2, CAP], F32R)
        act_b = z("act_b", [P, FT, CAP], BF16)
        x_hl = z("x_hl", [P, KT, 2, CAP], F32R)
        x_b = z("x_b", [P, KT, CAP], BF16)
        x_f = z("x_f", [P, KT, CAP])
        act_f = [z(f"act_f{u}", [P, 2, CAP]) for u in range(2)]
        gu = [z(f"gu{u}", [P, 2, CAP]) for u in range(2)]
        lows = [z("lows0", [P, 2, CAP])]
        lows_at = Z[0]
        lows.append(z("lows1", [P, 2, CAP]))
        y_low = [at(f"y_low{u}", [P, CAP], lows_at + 4 * CAP * u) for u in range(2)]
        yT = [at(f"yT{u}", [P, CAP], early_at + 4 * CAP * u) for u in range(2)]
        silu = [z(f"silu{u}", [P, CAP]) for u in range(2)]
        assert Z[0] <= nc.sbuf_usable_end

        ps = ctx.enter_context(nc.psum_tensor("ps", [P, 8 * BANK], F32))

        def bank(b, n=BANK, parts=slice(0, P), first=0):
            return ps[parts, b * BANK + first:b * BANK + first + n]

        def gate_up(b):
            return ps[:, b * BANK:(b + 2) * BANK].rearrange("p (g n) -> p g n", n=BANK)

        ident_ready = sem("ident_ready")
        ones_cleared = sem("ones_cleared")
        CONSTS = 6
        const_ready = sem("const_ready")
        small_loaded = sem("small_loaded")
        pad_ready = sem("pad_ready")
        pad_loaded = sem("pad_loaded")
        skew_stored = sem("skew_stored")
        mask_loaded = sem("mask_loaded")
        a_loaded = [sem(f"a_loaded{u}") for u in range(2)]
        a_stat = sem("a_stat")
        a_norm = sem("a_norm")
        a_tr = sem("a_tr")
        a_out = sem("a_out")
        f_tables = sem("f_tables")
        f_loaded = sem("f_loaded")
        f_proj = sem("f_proj")
        f_copied = sem("f_copied")
        f_chan = sem("f_chan")
        f_mixed = sem("f_mixed")
        f_pos = sem("f_pos")
        f_out = sem("f_out")
        h_loaded = sem("h_loaded")
        b_loaded = sem("b_loaded")
        b_step = sem("b_step")
        h_proj = sem("h_proj")
        h_sq = sem("h_sq")
        h_ss = sem("h_ss")
        h_ln = sem("h_ln")
        h_rinv = sem("h_rinv")
        h_qk = sem("h_qk")
        h_vT = sem("h_vT")
        h_vtr = sem("h_vtr")
        h_v = sem("h_v")
        s_ready = sem("s_ready")
        s_added = sem("s_added")
        s_max = sem("s_max")
        p_exp = sem("p_exp")
        p_rec = sem("p_rec")
        p_ready = sem("p_ready")
        p_tr = sem("p_tr")
        p_copied = sem("p_copied")
        pv_done = sem("pv_done")
        o_out = sem("o_out")
        m_raw_loaded = [sem(f"m_raw_loaded{u}") for u in range(2)]
        m_w_loaded = [sem(f"m_w_loaded{u}") for u in range(2)]
        hx_high = sem("hx_high")
        hx_ready = sem("hx_ready")
        m_high = sem("m_high")
        m_split = sem("m_split")
        m_gate = sem("m_gate")
        m_branch = sem("m_branch")
        m_sig = sem("m_sig")
        m_mul = sem("m_mul")
        m_out = sem("m_out")
        wout_loaded = [sem(f"wout_loaded{n}") for n in range(4)]
        r_loaded = [sem(f"r_loaded{u}") for u in range(2)]
        o_tok = sem("o_tok")
        o_mm = sem("o_mm")
        o_x1 = sem("o_x1")
        o_stat = sem("o_stat")
        o_xn = sem("o_xn")
        o_tr = sem("o_tr")
        o_h2 = sem("o_h2")
        o_log = sem("o_log")
        o_logc = sem("o_logc")
        x1_stored = [sem(f"x1_stored{u}") for u in range(2)]
        xn_stored = [sem(f"xn_stored{u}") for u in range(2)]
        r_tr = sem("r_tr")
        r_dve = sem("r_dve")
        r_exp = sem("r_exp")
        raw_loaded = [sem(f"raw_loaded{s}") for s in range(RAW_SLOTS)]
        hi_ready = sem("hi_ready")
        lo_dve = sem("lo_dve")
        lo_pool = sem("lo_pool")
        first_units = sem("first_units")
        cols_ready = sem("cols_ready")
        rows_moved = sem("rows_moved")
        x_tr = sem("x_tr")
        xf_ready = sem("xf_ready")
        x_hi_ready = sem("x_hi_ready")
        x_ready = sem("x_ready")
        gu_ready = sem("gu_ready")
        low_ready = sem("low_ready")
        gu_added = sem("gu_added")
        silu_ready = sem("silu_ready")
        act_f_ready = sem("act_f_ready")
        act_hi_ready = sem("act_hi_ready")
        act_ready = sem("act_ready")
        down_ready = sem("down_ready")
        y_low_ready = sem("y_low_ready")
        yT_ready = sem("yT_ready")
        y_tr = sem("y_tr")
        y_ready = sem("y_ready")

        pool_passed, dve_passed, sp_passed = sem("pool_passed"), sem("dve_passed"), sem("sp_passed")

        def apart(engine, passed):
            engine.sem_inc(passed, 1)

        def wait_consumed(engine, e, v):
            if 0 <= v < 16:
                engine.wait_ge(gu_ready, e * FT + (v // 2 * 2 + 2))
            else:
                engine.wait_ge(down_ready, e * KT + (v % UNITS - 16 + 1 + (KT if v >= 0 else 0)))

        def wait_split(engine, e, v):
            if v in POOLS:
                engine.wait_ge(lo_pool, e * len(POOLS) + (POOLS.index(v) + 1))
            else:
                engine.wait_ge(lo_dve, e * len(DVES) + (DVES.index(v) + 1))

        def raw_half(v):
            c, half = place_of(v)
            n = 256 if v < 16 else 128
            return raw[c % RAW_SLOTS][:, :].rearrange("p (k n) -> p k n", n=2 * n)[:, :, n * half:n * half + n]

        def unit(ring, v):
            return ring[v % UNIT_SLOTS][:, :].rearrange("p (k n) -> p k n", n=256 if v < 16 else 128)

        def low_part(engine, e, v, signal):
            engine.wait_ge(hi_ready, e * UNITS + (v + 1))
            v %= UNITS
            engine.tensor_tensor(unit(w_lo, v), raw_half(v), unit(w_hi, v).bitcast(F32), ALU.subtract)\
                  .then_inc(signal, 1)

        block = ctx.enter_context(nc.Block())

        @block.sync
        def _(sp):
            ts = bass.ts
            sp.dma_start(g1_sb[:, :], g1).then_inc(small_loaded, 16)
            sp.dma_start(g2_sb[:, :], g2).then_inc(small_loaded, 16)
            for n, g in enumerate((q_g, k_g)):
                for half in range(2):
                    sp.dma_start(qk_g[DH * half:DH * half + DH, n:n + 1], g.rearrange("(p o) -> p o", o=1))\
                      .then_inc(small_loaded, 16)
            sp.dma_start(wr_sb[:, :, :], w_r.rearrange("(k p) e -> p k e", p=P)).then_inc(small_loaded, 16)
            for u in range(2):
                sp.dma_start(x_in[u][:, :], x[u * P:u * P + P, :]).then_inc(a_loaded[u], 16)
            with sp.Fori(0, NT // 2 - 1) as i:
                for u in range(2):
                    sp.wait_ge(a_norm, i * 2 + u + 1)
                    sp.dma_start(x_in[u][:, :], x[ts(i * 2 + u + 2, P), :]).then_inc(a_loaded[u], 16)
            sp.wait_ge(a_norm, NT)
            sp.wait_ge(a_tr, NT)
            sp.dma_start(f_w[:, :, :], w_in[:, F_COL:F_COL + FD].rearrange("(k p) n -> p k n", p=P))\
              .then_inc(f_loaded, 16)
            sp.dma_start(dft_sb[:, :], dft_c).then_inc(f_tables, 16)
            sp.dma_start(pos_c_sb[:, :, :], pos_c.rearrange("(k p) n -> p k n", p=P)).then_inc(f_tables, 16)
            sp.dma_start(pos_s_sb[:, :, :], pos_s.rearrange("(k p) n -> p k n", p=P)).then_inc(f_tables, 16)
            sp.dma_start(spos_c_sb[:, :, :], spos_c.rearrange("(k p) n -> p k n", p=P)).then_inc(f_tables, 16)
            sp.dma_start(spos_s_sb[:, :, :], spos_s.rearrange("(k p) n -> p k n", p=P)).then_inc(f_tables, 16)
            with sp.Fori(0, FG - 1) as g:
                sp.wait_ge(f_proj, g * 3 + 3)
                sp.dma_start(f_w[:, :, :], w_in[:, bass.ds(g * FD + (F_COL + FD), FD)]
                             .rearrange("(k p) n -> p k n", p=P)).then_inc(f_loaded, 16)

            def head_loads(hp):
                for n in range(3):
                    sp.dma_start(h_w[:, n, :, :], w_in[:, bass.ds(hp * P + n * NA, P)]
                                 .rearrange("(k p) n -> p k n", p=P)).then_inc(h_loaded, 16)

            def bias_loads(hp):
                for hh in range(2):
                    for ri in range(2):
                        rows = skew[bass.ds((hp * 2 + hh) * RPB_H + (1 - ri), BIAS_ROWS), :, :]
                        src = bass.AP(rows.tensor, rows.offset + (GRID - 1),
                                      [[SKEW - 1, GRID], [GRID * SKEW, BIAS_ROWS], [1, GRID]])
                        sp.dma_start(bias_raw[GRID * ri:GRID * ri + GRID, hh, :, :], src).then_inc(b_loaded, 16)

            head_loads(0)
            sp.wait_ge(skew_stored, 16)
            bias_loads(0)
            with sp.Fori(1, HEADS // 2) as hp:
                sp.wait_ge(h_proj, hp * 9)
                head_loads(hp)
                sp.wait_ge(b_step, hp * 8 - 6)
                bias_loads(hp)

            def load_gate(m, u):
                sp.dma_start(m_raw[u][:, :, :], w_in[:, bass.ds(m * P + (GA_COL, GF_COL)[u], P)]
                             .rearrange("(k p) n -> p k n", p=P)).then_inc(m_raw_loaded[u], 16)

            def load_branch(m, u):
                sp.dma_start(m_w[u][:, :, :], (w_na, w_fo)[u][:, bass.ds(m * P, P)]
                             .rearrange("(k p) n -> p k n", p=P)).then_inc(m_w_loaded[u], 16)

            sp.wait_ge(h_proj, HEADS // 2 * 9)
            sp.wait_ge(b_step, HEADS // 2 * 8)
            for u in range(2):
                load_gate(0, u)
                load_branch(0, u)
            with sp.Fori(0, KT - 1) as m:
                for u in range(2):
                    sp.wait_ge(m_split, m * 2 + (u + 1))
                    apart(sp, sp_passed)
                    load_gate(m + 1, u)
                for u in range(2):
                    sp.wait_ge(m_branch, m * 6 + (3 * u + 3))
                    apart(sp, sp_passed)
                    load_branch(m + 1, u)

            def expert_load(e, c):
                s = c % RAW_SLOTS
                n = 512 if c < 8 else 256
                w, col = ((w_g, w_u)[c % 2], c // 2 * n) if c < 8 else (w_d, (c - 8) * n)
                sp.dma_start(raw[s][:, :].rearrange("p (k n) -> p k n", n=n),
                             w[bass.ds(e, 1), :, col:col + n].rearrange("a (k p) n -> p (a k) n", p=P))\
                  .then_inc(raw_loaded[s], 16)

            sp.wait_ge(m_out, len(CHUNKS) * KT)
            for u in range(2):
                sp.dma_start(x_res[u][:, :], x[u * P:u * P + P, :]).then_inc(r_loaded[u], 16)
            for n in range(4):
                sp.dma_start(w_out_sb[:, 2 * n:2 * n + 2, :], w_out[2 * P * n:2 * P * n + 2 * P, :]
                             .rearrange("(k p) n -> p k n", p=P)).then_inc(wout_loaded[n], 16)
            for c in range(RAW_SLOTS):
                expert_load(0, c)

            def store_x1(t, u, n):
                sp.wait_ge(o_x1, t + 1)
                sp.dma_start(y[ts(t, P), :], x1[u][:, :]).then_inc(x1_stored[u], 16)

            def store_xn(t, u, n):
                sp.wait_ge(o_xn, t + 1)
                sp.dma_start(xn_dram[ts(t, P), :], xn[u][:, :]).then_inc(xn_stored[u], 16)

            with sp.Fori(0, NT // 2 - 1) as i:
                for u in range(2):
                    store_x1(i * 2 + u, u, i)
                    sp.dma_start(x_res[u][:, :], x[ts(i * 2 + (u + 2), P), :]).then_inc(r_loaded[u], 16)
                    store_xn(i * 2 + u, u, i)
            for u in range(2):
                store_x1(NT - 2 + u, u, 0)
                store_xn(NT - 2 + u, u, 0)
            def wait_chunk_split(e, c):
                for v in range(UNITS):
                    if place_of(v)[0] == c:
                        wait_split(sp, e, v)
                        apart(sp, sp_passed)

            sp.wait_ge(first_units, LEAD)
            with sp.Fori(0, EXPERTS - 1) as e:
                for c in range(CHUNKS_E):
                    wait_chunk_split(e, c)
                    n = c + RAW_SLOTS
                    expert_load(e + n // CHUNKS_E, n % CHUNKS_E)
            for c in range(CHUNKS_E - RAW_SLOTS):
                wait_chunk_split(EXPERTS - 1, c)
                expert_load(EXPERTS - 1, c + RAW_SLOTS)
            for c in range(2):
                sp.wait_ge(raw_loaded[c], 16 * 3 * EXPERTS)
                sp.sem_inc(raw_loaded[c], 16)
            for u in range(2):
                sp.wait_ge(x1_stored[u], 16 * (NT // 2))
                sp.wait_ge(xn_stored[u], 16 * (NT // 2))
            sp.wait_ge(rows_moved, 64 * EXPERTS + 32)

        @block.gpsimd
        def _(pool):
            pool.memset(ident[:, :], 0.0).then_inc(ident_ready, 1)
            pool.memset(eps[:, :], EPS).then_inc(const_ready, 1)
            pool.wait_ge(ident_ready, 1)
            pool.affine_select(out=ident[:, :], in_=ident[:, :], compare_op=ALU.not_equal, fill=1.0,
                               base=0, pattern=[[-1, P]], channel_multiplier=1).then_inc(ident_ready, 1)
            pool.memset(idx_t[:, :, :], 0).then_inc(const_ready, 1)
            pool.memset(gate_t[:, :, :], 0.0).then_inc(const_ready, 1)
            pool.memset(rpb_pad[:, :], 0.0).then_inc(pad_ready, 1)
            pool.wait_ge(pad_ready, 1)
            pool.dma_start(rpb_pad[:, GRID - KW:GRID - KW + RPB_W], rpb.rearrange("h j x -> (h j) x"))\
                .then_inc(pad_loaded, 16)
            pool.wait_ge(pad_loaded, 16)
            pool.dma_start(skew, rpb_pad[:, :].rearrange("q (o x) -> q o x", o=1)
                           .broadcast_to([HEADS * RPB_H, GRID, SKEW])).then_inc(skew_stored, 16)
            pool.dma_start(mask_sb[:, :], col_mask).then_inc(mask_loaded, 16)
            pool.wait_ge(mask_loaded, 16)
            pool.wait_ge(f_out, 3 * FG)
            mask_b = mask_sb[:, :].rearrange("p (o x) -> p o x", o=1)
            with pool.Fori(0, HEADS // 2) as hp:
                pool.wait_ge(b_loaded, hp * 64 + 64)
                pool.wait_ge(o_out, hp * NT + 1)
                for hh in range(2):
                    pool.tensor_tensor(bias_all[:, hh, :, :], bias_raw[:, hh, :, :],
                                       mask_b.broadcast_to([P, BIAS_ROWS, GRID]), ALU.add).then_inc(b_step, 1)
                pool.wait_ge(b_step, hp * 8 + 2)
                apart(pool, pool_passed)
                for hh in range(2):
                    first = KH - 2 - KH // 2
                    pool.tensor_copy(bias_in[:, hh, :, :], bias_all[:, hh, first:first + INNER_ROWS, :])\
                        .then_inc(b_step, 1)
                pool.wait_ge(b_step, hp * 8 + 4)
                apart(pool, pool_passed)
                for hh in range(2):
                    pool.memset(bias_in[0:GRID, hh, INNER_ROWS - 1, :], MASKED).then_inc(b_step, 1)
                    pool.memset(bias_in[GRID:P, hh, 0, :], MASKED).then_inc(b_step, 1)
            pool.wait_ge(b_step, HEADS // 2 * 8)
            pool.wait_ge(h_proj, HEADS // 2 * 9)
            for c, (c0, cn) in enumerate(CHUNKS):
                pool.tensor_copy(hx_hi[c][:, :, :], hT[:, :, c0:c0 + cn]).then_inc(hx_high, 1)
                pool.wait_ge(hx_high, c + 1)
                pool.tensor_tensor(hx_lo[:, :, c0:c0 + cn], hT[:, :, c0:c0 + cn], hx_hi[c][:, :, :].bitcast(F32),
                                   ALU.subtract).then_inc(hx_ready, 1)
                pool.wait_ge(hx_ready, c + 1)
            with pool.Fori(0, KT) as m:
                for u in range(2):
                    pool.wait_ge(m_raw_loaded[u], m * 16 + 16)
                    apart(pool, pool_passed)
                    pool.wait_ge(m_gate, m * 6 + (3 * u + 3))
                    apart(pool, pool_passed)
                    pool.tensor_copy(m_hi[u][:, :, :], m_raw[u][:, :, :]).then_inc(m_high, 1)
                    pool.wait_ge(m_high, m * 2 + (u + 1))
                    pool.tensor_tensor(m_lo[u][:, :, :], m_raw[u][:, :, :], m_hi[u][:, :, :].bitcast(F32),
                                       ALU.subtract).then_inc(m_split, 1)
                    pool.wait_ge(m_split, m * 2 + (u + 1))
                    apart(pool, pool_passed)
            pool.sem_inc(lo_pool, sum(v in POOLS for v in range(LEAD)))
            for v in range(LEAD):
                low_part(pool, 0, v, first_units)
            pool.wait_ge(cols_ready, 1)
            for u in range(2):
                pool.wait_ge(xn_stored[u], 16 * (NT // 2))
                pool.wait_ge(x1_stored[u], 16 * (NT // 2))
            xg_count = sem("gather_cols")
            sc_count = sem("scatter_cols")

            def gather(n):
                pool.tensor_copy(idx_gather[:, :], idx_t[:, :, bass.ds(n, 1)].rearrange("p a b -> p (a b)"))\
                    .then_inc(xg_count, 1)
                pool.wait_ge(xg_count, n + 1)
                apart(pool, pool_passed)
                pool.indirect_dma_start(xg_p[:, :], None, xn_dram,
                                        bass.IndirectOffsetOnAxis(idx_gather[:, 0:1], 0)).then_inc(rows_moved, 16)
                pool.indirect_dma_start(xg_s[:, :], None, xn_dram,
                                        bass.IndirectOffsetOnAxis(idx_gather[0:CAP_S, 1:2], 0))\
                    .then_inc(rows_moved, 16)

            def lows(e, step):
                for v in ahead(step):
                    if v % UNITS in POOLS:
                        low_part(pool, e, v, lo_pool)

            gather(0)
            with pool.Fori(0, EXPERTS) as e:
                lows(e, 0)
                pool.wait_ge(x_tr, e + 1)
                gather(e + 1)
                for step in range(1, 4):
                    lows(e, step)
                pool.wait_ge(rows_moved, e * 64 + 64)
                pool.tensor_copy(idx_scatter[:, :], idx_t[:, :, bass.ds(e, 1)].rearrange("p a b -> p (a b)"))\
                    .then_inc(sc_count, 1)
                pool.tensor_copy(gate_now[:, :], gate_t[:, :, bass.ds(e, 1)].rearrange("p a b -> p (a b)"))\
                    .then_inc(sc_count, 1)
                pool.wait_ge(sc_count, e * 2 + 2)
                pool.sem_inc(cols_ready, 1)
                for step in range(4, 16):
                    lows(e, step)
                pool.wait_ge(y_ready, e * 4 + 5)
                apart(pool, pool_passed)
                pool.indirect_dma_start(y, bass.IndirectOffsetOnAxis(idx_scatter[:, 0:1], 0), ye_p[:, :], None,
                                        compute_op=ALU.add).then_inc(rows_moved, 16)
                pool.indirect_dma_start(y, bass.IndirectOffsetOnAxis(idx_scatter[0:CAP_S, 1:2], 0),
                                        ye_s[:, :], None, compute_op=ALU.add).then_inc(rows_moved, 16)
            pool.wait_ge(rows_moved, 64 * EXPERTS + 32)

        @block.scalar
        def _(act):
            act.preload_act_table_set("natural_log_exp_and_others")
            act.wait_ge(const_ready, CONSTS)

            def inv_rms(step, n, src, u, length):
                act.wait_ge(step, n + 1)
                act.activation(lnv[:, u:u + 1], src, ACT.Ln, bias=eps[:, 0:1], scale=1.0 / length)\
                   .then_inc(step, 1)
                act.wait_ge(step, n + 2)
                act.activation(rstd[:, u:u + 1], lnv[:, u:u + 1], ACT.Exp, scale=-0.5).then_inc(step, 1)

            with act.Fori(0, NT // 2) as i:
                for u in range(2):
                    n = (i * 2 + u) * 3
                    act.wait_ge(a_loaded[u], i * 16 + 16)
                    act.activation(junk_a[:, :], x_in[u][:, :], ACT.Square, accum_out=ss[:, u:u + 1])\
                       .then_inc(a_stat, 1)
                    inv_rms(a_stat, n, ss[:, u:u + 1], u, D)
            with act.Fori(0, FG) as g:
                for c, (c0, cn) in enumerate(CHUNKS):
                    act.wait_ge(f_proj, g * 3 + (c + 1))
                    act.activation(fT[:, c0:c0 + cn], bank(c, cn), ACT.Copy).then_inc(f_copied, 1)
            with act.Fori(0, HEADS // 2) as hp:
                def rinv_of(j):
                    cn = CHUNKS[j % 3][1]
                    act.wait_ge(h_ss, hp * 6 + (j + 1))
                    if j >= 2:
                        act.wait_ge(h_qk, hp * 6 + (j - 1))
                    act.activation(rinv[j % 2][:, 0:cn], bank(3 + j % 2, cn), ACT.Ln, bias=eps[:, 0:1],
                                   scale=1.0 / DH).then_inc(h_ln, 1)
                    act.wait_ge(h_ln, hp * 6 + (j + 1))
                    act.activation(rinv[j % 2][:, 0:cn], rinv[j % 2][:, 0:cn], ACT.Exp, scale=-0.5)\
                       .then_inc(h_rinv, 1)

                for j in range(9):
                    c0, cn = CHUNKS[j % 3]
                    act.wait_ge(h_proj, hp * 9 + (j + 1))
                    if j < 6:
                        if j >= 2:
                            act.wait_ge(h_ss, hp * 6 + (j - 1))
                        act.activation(sq[j % 2][:, 0:cn], bank(j % 3, cn), ACT.Square).then_inc(h_sq, 1)
                    else:
                        act.activation(qkvT[:, 2, c0:c0 + cn], bank(j % 3, cn), ACT.Copy).then_inc(h_vT, 1)
                    if 1 <= j < 7:
                        rinv_of(j - 1)

                def exponent(j):
                    nk = TILES[j // 2][1] * GRID
                    act.wait_ge(s_max, hp * 20 + (j + 1))
                    u = j % P_SLOTS
                    act.activation(p_sb[u][:, 0:nk], p_sb[u][:, 0:nk], ACT.Exp,
                                   bias=neg_max[:, u:u + 1], accum_out=row_sum[:, u:u + 1])\
                       .then_inc(p_exp, 1)

                exponent(0)
                exponent(1)
                for j in range(20):
                    if j < 18:
                        exponent(j + 2)
                    nk = TILES[j // 2][1] * GRID
                    full = min(nk // P, 4)
                    act.wait_ge(p_tr, hp * 20 + (j + 1))
                    if j >= 2:
                        act.wait_ge(pv_done, hp * 20 + (j - 1))
                    if nk > 4 * P:
                        act.activation(pT[j % 2][0:GRID, 4, :], bank(3, P, slice(0, GRID)), ACT.Copy)
                    act.activation(pT[j % 2][:, 0:full, :], bank(2, full * P).rearrange("p (k n) -> p k n", n=P),
                                   ACT.Copy).then_inc(p_copied, 1)
            act.preload_act_table(ACT.Sigmoid)
            with act.Fori(0, KT) as m:
                for u in range(2):
                    for c, (c0, cn) in enumerate(CHUNKS):
                        q = 3 * u + c
                        act.wait_ge(m_mul, m * 6 + (q + 1))
                        act.wait_ge(m_gate, m * 6 + (q + 7))
                        act.activation(sig[u][:, c0:c0 + cn], bank(q, cn), ACT.Sigmoid).then_inc(m_sig, 1)
            act.preload_act_table_set("natural_log_exp_and_others")
            with act.Fori(0, NT // 2) as i:
                for u in range(2):
                    n = (i * 2 + u) * 3
                    act.wait_ge(o_x1, i * 2 + (u + 1))
                    act.activation(junk_o[:, :], x1[u][:, :], ACT.Square, accum_out=ss[:, u:u + 1])\
                       .then_inc(o_stat, 1)
                    inv_rms(o_stat, n, ss[:, u:u + 1], u, D)
            act.wait_ge(r_dve, 3)
            act.activation(aff_tok[:, :, :], log_tok[:, :, :], ACT.Exp).then_inc(r_exp, 1)
            act.preload_act_table(ACT.Silu)

            def high_part(e, v, first=False):
                n, w = v // UNITS, v % UNITS
                c = place_of(w)[0]
                act.wait_ge(raw_loaded[c % RAW_SLOTS], e * 48 + 16 * (3 * n + c // RAW_SLOTS + 1))
                if not first:
                    wait_consumed(act, e, v - UNIT_SLOTS)
                act.activation(unit(w_hi, w), raw_half(w), ACT.Copy).then_inc(hi_ready, 1)

            act.wait_ge(o_mm, NT)
            for v in range(LEAD):
                high_part(0, v, first=True)

            def token_high(n):
                act.wait_ge(xf_ready, n + 1)
                act.activation(x_hl[:, :, 0, :], x_f[:, :, :], ACT.Copy).then_inc(x_hi_ready, 1)

            token_high(0)
            with act.Fori(0, EXPERTS) as e:
                def low_sums(j):
                    b = 2 * (j % 2)
                    act.wait_ge(gu_ready, e * FT + (j + 1))
                    if j >= 2:
                        act.wait_ge(gu_added, e * FT + (j - 1))
                    act.activation(lows[j % 2][:, :, :], gate_up(b)[:, :, CAP:2 * CAP], ACT.Copy)\
                       .then_inc(low_ready, 1)

                def gate(j):
                    act.wait_ge(gu_added, e * FT + (j + 1))
                    if j >= 2:
                        act.wait_ge(act_f_ready, e * FT + (j - 1))
                    act.activation(silu[j % 2][:, :], gu[j % 2][:, 0, :], ACT.Silu).then_inc(silu_ready, 1)

                def act_high(pair):
                    act.wait_ge(act_f_ready, e * FT + (2 * pair + 2))
                    act.activation(act_hl[:, 2 * pair:2 * pair + 2, 0, :], act_f[pair % 2][:, :, :], ACT.Copy)\
                       .then_inc(act_hi_ready, 1)

                def y_lows(d):
                    act.wait_ge(down_ready, e * KT + (KT + d + 1))
                    if d >= 2:
                        act.wait_ge(yT_ready, e * KT + (d - 1))
                    act.activation(y_low[d % 2][:, :], bank(4 + d % 2, CAP, first=CAP), ACT.Copy)\
                       .then_inc(y_low_ready, 1)

                for step in range(8):
                    if step:
                        low_sums(2 * step - 1)
                    high_part(e, ahead(step)[0])
                    if step:
                        gate(2 * step - 1)
                    low_sums(2 * step)
                    high_part(e, ahead(step)[1])
                    if step:
                        act_high(step - 1)
                    gate(2 * step)
                low_sums(FT - 1)
                gate(FT - 1)
                act_high(7)
                for d in range(KT):
                    high_part(e, ahead(8 + d)[0])
                    y_lows(d)
                    if d == 1:
                        token_high(e + 1)

        @block.vector
        def _(dve):
            dve.sem_inc(o_out, 1)
            dve.sem_inc(m_mul, 6)
            dve.sem_inc(y_ready, 1)

            def times_gain(out, src, gain, inner):
                return dve.tensor_tensor(out, src, gain.rearrange("p (k o) -> p k o", o=1)
                                         .broadcast_to([P, gain.shape[1], inner]), ALU.mult)

            dve.memset(head_ones[:, :], 0.0).then_inc(ones_cleared, 1)
            for half in range(2):
                a = DH * half
                dve.wait_ge(ones_cleared, 1)
                dve.memset(head_ones[a:a + DH, a:a + DH], 1.0).then_inc(const_ready, 1)
            dve.wait_ge(small_loaded, 16 * 7)
            dve.tensor_scalar(qk_g[:, 0:1], qk_g[:, 0:1], DH ** -0.5, None, ALU.mult).then_inc(const_ready, 1)
            with dve.Fori(0, NT // 2) as i:
                for u in range(2):
                    dve.wait_ge(a_stat, i * 6 + (3 * u + 3))
                    dve.tensor_scalar(xn_a[u][:, :], x_in[u][:, :], rstd[:, u:u + 1], None, ALU.mult)\
                       .then_inc(a_norm, 1)
                for u in range(2):
                    dve.wait_ge(a_tr, i * 2 + (u + 1))
                    times_gain(hT[:, :, bass.ts(i * 2 + u, P)], ps[:, 1024 * u:1024 * u + 1024]
                               .rearrange("p (k n) -> p k n", n=P), g1_sb[:, :], P).then_inc(a_out, 1)
            with dve.Fori(0, FG) as g:
                for pair in range(NT // 2):
                    dve.wait_ge(f_chan, g * 5 + (pair + 1))
                    dve.tensor_copy(f_mix[:, 2 * pair:2 * pair + 2, :],
                                    bank(3 + pair % 2).rearrange("p (t n) -> p t n", n=2 * FD))\
                       .then_inc(f_mixed, 1)
                for c, (c0, cn) in enumerate(CHUNKS):
                    dve.wait_ge(f_pos, g * 3 + (c + 1))
                    dve.tensor_scalar(ofT[:, bass.ds(g, 1), c0:c0 + cn],
                                      bank(5 + c, cn).rearrange("p (o n) -> p o n", o=1), 1.0, None, ALU.mult)\
                       .then_inc(f_out, 1)
            dve.wait_ge(const_ready, CONSTS)
            with dve.Fori(0, HEADS // 2) as hp:
                for j in range(6):
                    n = j // 3
                    c0, cn = CHUNKS[j % 3]
                    dve.wait_ge(h_rinv, hp * 6 + (j + 1))
                    dve.scalar_tensor_tensor(qkvT[:, n, c0:c0 + cn], bank(j % 3, cn), qk_g[:, n:n + 1],
                                             rinv[j % 2][:, 0:cn], ALU.mult, ALU.mult).then_inc(h_qk, 1)
                for c, (c0, cn) in enumerate(CHUNKS):
                    dve.wait_ge(h_vtr, hp * 3 + (c + 1))
                    dve.tensor_copy(v_tok[:, c0 // P:(c0 + cn) // P, :],
                                    bank(3 + c % 2, cn).rearrange("p (t n) -> p t n", n=P)).then_inc(h_v, 1)

                def add_bias(j):
                    _, rows, row, inner = TILES[j // 2]
                    nk, u, b = rows * GRID, j % P_SLOTS, j % 2
                    table = bias_in[:, j % 2, :, :] if inner else bias_all[:, j % 2, row:row + rows, :]
                    dve.wait_ge(s_ready, hp * 20 + (j + 1))
                    if j == 0:
                        dve.wait_ge(b_step, hp * 8 + 8)
                    if j >= P_SLOTS:
                        dve.wait_ge(p_tr, hp * 20 + (j - P_SLOTS + 1))
                    apart(dve, dve_passed)
                    dve.tensor_tensor_reduce(
                        out=p_sb[u][:, 0:nk], in0=ps[:, 2048 + 1024 * b:2048 + 1024 * b + nk],
                        in1=table.rearrange("p r c -> p (r c)"), scale=1.0, scalar=-3.0e38,
                        op0=ALU.add, op1=ALU.max, accum_out=row_max[:, u:u + 1]).then_inc(s_added, 1)
                    dve.wait_ge(s_added, hp * 20 + (j + 1))
                    dve.tensor_scalar(neg_max[:, u:u + 1], row_max[:, u:u + 1], -1.0, None, ALU.mult)\
                       .then_inc(s_max, 1)

                def normalise(j):
                    nk, u = TILES[j // 2][1] * GRID, j % P_SLOTS
                    dve.wait_ge(p_exp, hp * 20 + (j + 1))
                    dve.reciprocal(row_rec[:, u:u + 1], row_sum[:, u:u + 1]).then_inc(p_rec, 1)
                    dve.wait_ge(p_rec, hp * 20 + (j + 1))
                    dve.tensor_scalar(p_sb[u][:, 0:nk], p_sb[u][:, 0:nk], row_rec[:, u:u + 1], None, ALU.mult)\
                       .then_inc(p_ready, 1)

                def attended(t):
                    dve.wait_ge(pv_done, hp * 20 + (2 * t + 2))
                    dve.tensor_scalar(onaT[:, bass.ds(hp, 1), P * t:P * t + P],
                                      bank(t % 2, P).rearrange("p (o n) -> p o n", o=1), 1.0, None, ALU.mult)\
                       .then_inc(o_out, 1)

                add_bias(0)
                add_bias(1)
                for j in range(20):
                    normalise(j)
                    if j >= 3 and j % 2:
                        attended((j - 3) // 2)
                    if j < 18:
                        add_bias(j + 2)
                attended(NT - 1)
            with dve.Fori(0, KT) as m:
                for c, (c0, cn) in enumerate(CHUNKS):
                    dve.wait_ge(m_sig, m * 6 + (c + 1))
                    dve.wait_ge(m_branch, m * 6 + (c + 1))
                    dve.tensor_tensor(mT[:, bass.ds(m, 1), c0:c0 + cn],
                                      sig[0][:, c0:c0 + cn].rearrange("p (o n) -> p o n", o=1),
                                      bank(BRANCH_BANKS[c], cn).rearrange("p (o n) -> p o n", o=1), ALU.mult)\
                       .then_inc(m_mul, 1)
                for c, (c0, cn) in enumerate(CHUNKS):
                    dve.wait_ge(m_sig, m * 6 + (c + 4))
                    dve.wait_ge(m_branch, m * 6 + (c + 4))
                    dve.tensor_tensor(gated[c % 2][:, 0:cn], sig[1][:, c0:c0 + cn], bank(BRANCH_BANKS[3 + c], cn),
                                      ALU.mult).then_inc(m_mul, 1)
                    dve.wait_ge(m_mul, m * 6 + (c + 10))
                    mc = mT[:, bass.ds(m, 1), c0:c0 + cn]
                    dve.tensor_tensor(mc, gated[c % 2][:, 0:cn].rearrange("p (o n) -> p o n", o=1), mc, ALU.add)\
                       .then_inc(m_out, 1)
                dve.wait_ge(m_out, m * 3 + 3)
                apart(dve, dve_passed)

            def token_slice(t, u, free):
                if free is not None:
                    dve.wait_ge(o_mm, free)
                dve.tensor_scalar(m_tok[u][:, :, :], mT[:, :, bass.ts(t, P)], 1.0, None, ALU.mult)\
                   .then_inc(o_tok, 1)

            def residual(t, u, i, free):
                dve.wait_ge(o_mm, t + 1)
                dve.wait_ge(r_loaded[u], i * 16 + 16)
                if free:
                    dve.wait_ge(x1_stored[u], i * 16)
                    dve.wait_ge(o_xn, t - 1)
                dve.tensor_tensor(x1[u][:, :], ps[:, 1024 * u:1024 * u + 1024], x_res[u][:, :], ALU.add)\
                   .then_inc(o_x1, 1)

            def normed(t, u, i, free):
                dve.wait_ge(o_stat, t * 3 + 3)
                if free:
                    dve.wait_ge(xn_stored[u], i * 16)
                    dve.wait_ge(o_tr, t - 1)
                dve.tensor_scalar(xn[u][:, :], x1[u][:, :], rstd[:, u:u + 1], None, ALU.mult).then_inc(o_xn, 1)

            def gained(t, u, free):
                dve.wait_ge(o_tr, t + 1)
                if free:
                    dve.wait_ge(o_log, t - 1)
                times_gain(h2T[u][:, :, :], ps[:, 2048 + 1024 * u:2048 + 1024 * u + 1024]
                           .rearrange("p (k n) -> p k n", n=P), g2_sb[:, :], P).then_inc(o_h2, 1)

            def logits(t, u):
                dve.wait_ge(o_log, t + 1)
                dve.tensor_scalar(logT[:, bass.ts(t, P)], bank(2 * u, P, slice(0, EXPERTS)), 1.0, None, ALU.mult)\
                   .then_inc(o_logc, 1)

            dve.wait_ge(m_out, len(CHUNKS) * KT)
            token_slice(0, 0, None)
            token_slice(1, 1, None)
            residual(0, 0, 0, False)
            normed(0, 0, 0, False)
            residual(1, 1, 0, False)
            token_slice(2, 0, 1)
            gained(0, 0, False)
            normed(1, 1, 0, False)
            logits(0, 0)
            with dve.Fori(0, NT // 2 - 2) as i:
                residual(i * 2 + 2, 0, i + 1, True)
                token_slice(i * 2 + 3, 1, i * 2 + 2)
                gained(i * 2 + 1, 1, False)
                normed(i * 2 + 2, 0, i + 1, True)
                logits(i * 2 + 1, 1)
                residual(i * 2 + 3, 1, i + 1, True)
                token_slice(i * 2 + 4, 0, i * 2 + 3)
                gained(i * 2 + 2, 0, True)
                normed(i * 2 + 3, 1, i + 1, True)
                logits(i * 2 + 2, 0)
            last = NT // 2 - 1
            residual(NT - 2, 0, last, True)
            token_slice(NT - 1, 1, NT - 2)
            gained(NT - 3, 1, True)
            normed(NT - 2, 0, last, True)
            logits(NT - 3, 1)
            residual(NT - 1, 1, last, True)
            gained(NT - 2, 0, True)
            normed(NT - 1, 1, last, True)
            logits(NT - 2, 0)
            gained(NT - 1, 1, True)
            logits(NT - 1, 1)

            count = [0]

            def step(instruction):
                count[0] += 1
                instruction.then_inc(r_dve, 1)
                dve.wait_ge(r_dve, count[0])

            def over_experts(a):
                return a.rearrange("p (t o) -> p t o", o=1).broadcast_to([P, NT, EXPERTS])

            dve.wait_ge(r_tr, 1)
            step(dve.tensor_copy(log_tok[:, :, :], bank(0, NT * EXPERTS).rearrange("p (t e) -> p t e", e=EXPERTS)))
            step(dve.reduce_max(r_max[:, :], log_tok[:, :, :], AX.X))
            step(dve.tensor_tensor(log_tok[:, :, :], log_tok[:, :, :], over_experts(r_max[:, :]), ALU.subtract))
            dve.wait_ge(r_exp, 1)
            step(dve.reduce_sum(r_sum[:, :], aff_tok[:, :, :], AX.X))
            step(dve.reciprocal(r_sum[:, :], r_sum[:, :]))
            step(dve.tensor_tensor(aff_tok[:, :, :], aff_tok[:, :, :], over_experts(r_sum[:, :]), ALU.mult))
            dve.wait_ge(r_tr, 2)
            step(dve.tensor_copy(aff[:, :], ps[0:EXPERTS, BANK:BANK + TOK]))
            for first, n, k0, cap in ((S_PROMPT, S_SAMPLE, CAP_P, CAP_S), (0, S_PROMPT, 0, CAP_P)):
                row = aff[:, first:first + n]
                for k in range(k0, k0 + cap, 8):
                    step(dve.max(top_v[:, k:k + 8], row))
                    step(dve.max_index(top_i[:, k:k + 8], top_v[:, k:k + 8], row))
                    if k + 8 < k0 + cap:
                        step(dve.match_replace(row, top_v[:, k:k + 8], row, -1.0))
            step(dve.tensor_copy(top_f[:, 0:CAP_P], top_i[:, 0:CAP_P]))
            step(dve.tensor_scalar(top_f[:, CAP_P:CAP], top_i[:, CAP_P:CAP], float(S_PROMPT), None, ALU.add))
            dve.sem_inc(r_exp, 1)
            dve.wait_ge(r_tr, 3)
            dve.tensor_copy(gate_t[:, 0, 0:EXPERTS], bank(0, EXPERTS))
            dve.tensor_copy(gate_t[0:CAP_S, 1, 0:EXPERTS], bank(0, EXPERTS, slice(0, CAP_S), EXPERTS))
            dve.tensor_copy(idx_t[:, 0, 0:EXPERTS], bank(0, EXPERTS, slice(0, P), 2 * EXPERTS))
            dve.tensor_copy(idx_t[0:CAP_S, 1, 0:EXPERTS], bank(0, EXPERTS, slice(0, CAP_S), 3 * EXPERTS))\
               .then_inc(cols_ready, 1)

            def expert_tokens(n):
                dve.wait_ge(x_tr, n + 1)
                for b, k0, kn in X_BANKS:
                    op = times_gain(x_f[:, k0:k0 + kn, :], bank(b, kn * CAP).rearrange("p (k n) -> p k n", n=CAP),
                                    g2_sb[:, k0:k0 + kn], CAP)
                op.then_inc(xf_ready, 1)
                dve.wait_ge(xf_ready, n + 1)
                dve.tensor_copy(x_b[:, :, :], x_f[:, :, :])

            def token_low(n):
                dve.wait_ge(x_hi_ready, n + 1)
                dve.tensor_tensor(x_hl[:, :, 1, :], x_f[:, :, :], x_hl[:, :, 0, :].bitcast(F32), ALU.subtract)\
                   .then_inc(x_ready, 1)

            dve.sem_inc(lo_dve, sum(v in DVES for v in range(LEAD)))
            expert_tokens(0)
            token_low(0)
            with dve.Fori(0, EXPERTS) as e:
                def split(v):
                    if v % UNITS in DVES:
                        low_part(dve, e, v, lo_dve)

                def add_lows(j):
                    dve.wait_ge(low_ready, e * FT + (j + 1))
                    dve.tensor_tensor(gu[j % 2][:, :, :], gate_up(2 * (j % 2))[:, :, 0:CAP], lows[j % 2][:, :, :],
                                      ALU.add).then_inc(gu_added, 1)

                def gated_up(j):
                    dve.wait_ge(silu_ready, e * FT + (j + 1))
                    if j >= 4 and j % 2 == 0:
                        dve.wait_ge(act_hi_ready, e * 8 + (j // 2 - 1))
                    dve.tensor_tensor(act_f[j // 2 % 2][:, j % 2, :], silu[j % 2][:, :], gu[j % 2][:, 1, :],
                                      ALU.mult).then_inc(act_f_ready, 1)

                def act_low(pair):
                    pairs = slice(2 * pair, 2 * pair + 2)
                    dve.wait_ge(act_f_ready, e * FT + (2 * pair + 2))
                    dve.tensor_copy(act_b[:, pairs, :], act_f[pair % 2][:, :, :])
                    dve.wait_ge(act_hi_ready, e * 8 + (pair + 1))
                    dve.tensor_tensor(act_hl[:, pairs, 1, :], act_f[pair % 2][:, :, :],
                                      act_hl[:, pairs, 0, :].bitcast(F32), ALU.subtract).then_inc(act_ready, 1)

                def add_y_lows(d):
                    dve.wait_ge(y_low_ready, e * KT + (d + 1))
                    if d >= 2:
                        dve.wait_ge(y_tr, e * KT + (d - 1))
                    dve.tensor_tensor(yT[d % 2][:, :], bank(4 + d % 2, CAP), y_low[d % 2][:, :], ALU.add)\
                       .then_inc(yT_ready, 1)

                def gated_rows(half):
                    p, q = Y_BANKS[half]
                    cols = slice(BANK * half, BANK * half + BANK)
                    dve.wait_ge(y_tr, e * KT + (4 * half + 4))
                    dve.tensor_scalar(ye_p[:, cols], bank(p), gate_now[:, 0:1], None, ALU.mult).then_inc(y_ready, 1)
                    dve.tensor_scalar(ye_s[:, cols], bank(q, BANK, slice(0, CAP_S)), gate_now[0:CAP_S, 1:2], None,
                                      ALU.mult).then_inc(y_ready, 1)

                for step in range(8):
                    if step:
                        add_lows(2 * step - 1)
                    split(ahead(step)[0])
                    if step:
                        gated_up(2 * step - 1)
                    add_lows(2 * step)
                    split(ahead(step)[1])
                    if step:
                        act_low(step - 1)
                    gated_up(2 * step)
                add_lows(FT - 1)
                gated_up(FT - 1)
                act_low(7)
                for d in range(KT):
                    split(ahead(8 + d)[0])
                    if d == 0:
                        expert_tokens(e + 1)
                    add_y_lows(d)
                    if d == 2:
                        token_low(e + 1)
                    if d == 4:
                        dve.wait_ge(cols_ready, e + 2)
                        gated_rows(0)
                gated_rows(1)

        @block.tensor
        def _(pe):
            def product(out, pairs):
                for n, (lhsT, rhs) in enumerate(pairs):
                    op = pe.matmul(out, lhsT, rhs, start=n == 0, stop=n == len(pairs) - 1)
                return op

            pe.wait_ge(const_ready, CONSTS)
            pe.wait_ge(ident_ready, 2)
            with pe.Fori(0, NT // 2) as i:
                for u in range(2):
                    pe.wait_ge(a_norm, i * 2 + (u + 1))
                    for k in range(KT):
                        op = pe.transpose(ps[:, 1024 * u + P * k:1024 * u + P * k + P],
                                          xn_a[u][:, P * k:P * k + P], ident[:, :])
                    op.then_inc(a_tr, 1)
            pe.wait_ge(a_out, NT)
            with pe.Fori(0, FG) as g:
                pe.wait_ge(f_loaded, g * 16 + 16)
                for c, (c0, cn) in enumerate(CHUNKS):
                    op = product(bank(c, cn), [(f_w[:, k, :], hT[:, k, c0:c0 + cn]) for k in range(KT)])
                    op.then_inc(f_proj, 1)
                pe.wait_ge(f_tables, 16 * 5)
                for pair in range(NT // 2):
                    pe.wait_ge(f_copied, g * 3 + (pair // 2 + 1))
                    if pair >= 2:
                        pe.wait_ge(f_mixed, g * 5 + (pair - 1))
                    for t in (2 * pair, 2 * pair + 1):
                        op = pe.matmul(bank(3 + pair % 2, 2 * FD, first=2 * FD * (t % 2)),
                                       fT[:, P * t:P * t + P], dft_sb[:, :], start=True, stop=True)
                    op.then_inc(f_chan, 1)
                pe.wait_ge(f_mixed, g * 5 + 5)
                for c, (c0, cn) in enumerate(CHUNKS):
                    prompt = c0 < S_PROMPT
                    tiles = range(PT_TILES) if prompt else range(PT_TILES, NT)
                    pairs = []
                    for t in tiles:
                        for half, table in enumerate((pos_c_sb, pos_s_sb) if prompt else (spos_c_sb, spos_s_sb)):
                            rhs = table[:, t, c0:c0 + cn] if prompt else table[:, t - PT_TILES, :]
                            pairs.append((f_mix[:, t, FD * half:FD * half + FD], rhs))
                    product(bank(5 + c, cn), pairs).then_inc(f_pos, 1)
            pe.wait_ge(f_out, 3 * FG)
            with pe.Fori(0, HEADS // 2) as hp:
                def sum_squares(j):
                    cn = CHUNKS[j % 3][1]
                    pe.wait_ge(h_sq, hp * 6 + (j + 1))
                    if j >= 2:
                        pe.wait_ge(h_ln, hp * 6 + (j - 1))
                    pe.matmul(bank(3 + j % 2, cn), head_ones[:, :], sq[j % 2][:, 0:cn], start=True, stop=True)\
                      .then_inc(h_ss, 1)

                def values(c):
                    c0, cn = CHUNKS[c]
                    pe.wait_ge(h_vT, hp * 3 + (c + 1))
                    if c == 0:
                        pe.wait_ge(h_ln, hp * 6 + 6)
                    if c == 2:
                        pe.wait_ge(h_v, hp * 3 + 1)
                    for t in range(cn // P):
                        op = pe.transpose(bank(3 + c % 2, P, first=P * t), qkvT[:, 2, c0 + P * t:c0 + P * t + P],
                                          ident[:, :])
                    op.then_inc(h_vtr, 1)

                pe.wait_ge(o_out, hp * NT + 1)
                pe.wait_ge(h_loaded, hp * 48 + 48)
                for j in range(9):
                    c0, cn = CHUNKS[j % 3]
                    if j >= 3:
                        pe.wait_ge(h_qk, hp * 6 + (j - 2))
                    product(bank(j % 3, cn), [(h_w[:, j // 3, k, :], hT[:, k, c0:c0 + cn]) for k in range(KT)])\
                        .then_inc(h_proj, 1)
                    if 1 <= j < 7:
                        sum_squares(j - 1)
                    if j >= 7:
                        values(j - 7)
                values(2)

                def scores(j):
                    t, hh = j // 2, j % 2
                    key0, rows, _, _ = TILES[t]
                    part = slice(DH * hh, DH * hh + DH)
                    at0 = 2048 + 1024 * (j % 2)
                    if j >= 2:
                        pe.wait_ge(s_added, hp * 20 + (j - 1))
                    n = min(rows * GRID, BANK)
                    op = pe.matmul(ps[:, at0:at0 + n], qkvT[part, 0, P * t:P * t + P],
                                   qkvT[part, 1, key0:key0 + n], start=True, stop=True)
                    if rows > KH:
                        op = pe.matmul(ps[:, at0 + n:at0 + n + P], qkvT[part, 0, P * t:P * t + P],
                                       qkvT[part, 1, key0 + n:key0 + n + P], start=True, stop=True)
                    op.then_inc(s_ready, 1)

                def transposed(j):
                    nk = TILES[j // 2][1] * GRID
                    pe.wait_ge(p_ready, hp * 20 + (j + 1))
                    if j >= 1:
                        pe.wait_ge(p_copied, hp * 20 + j)
                    for k in range(min(nk // P, 4)):
                        op = pe.transpose(bank(2, P, first=P * k), p_sb[j % P_SLOTS][:, P * k:P * k + P], ident[:, :])
                    if nk > 4 * P:
                        op = pe.transpose(bank(3, P, slice(0, GRID)), p_sb[j % P_SLOTS][:, 4 * P:nk], ident[:, :])
                    op.then_inc(p_tr, 1)

                def attend(j):
                    t, hh = j // 2, j % 2
                    key0, rows, _, _ = TILES[t]
                    first, nk = key0 // P, rows * GRID
                    cols = slice(DH * hh, DH * hh + DH)
                    pe.wait_ge(p_copied, hp * 20 + (j + 1))
                    if t >= 2:
                        pe.wait_ge(o_out, hp * NT + t)
                    pairs = [(v_tok[:, first + k, cols], pT[j % 2][:, k, :]) for k in range(min(nk // P, 4))]
                    if nk > 4 * P:
                        pairs.append((v_tok[0:GRID, first + 4, cols], pT[j % 2][0:GRID, 4, :]))
                    product(bank(t % 2, P, cols), pairs).then_inc(pv_done, 1)

                pe.wait_ge(h_qk, hp * 6 + 6)
                pe.wait_ge(h_v, hp * 3 + 3)
                scores(0)
                scores(1)
                for j in range(20):
                    if j < 18:
                        scores(j + 2)
                    transposed(j)
                    if j >= 1:
                        attend(j - 1)
                attend(19)
            pe.wait_ge(o_out, HEADS // 2 * NT + 1)
            pe.sem_inc(m_gate, 6)
            pe.wait_ge(hx_ready, len(CHUNKS))
            with pe.Fori(0, KT) as m:
                for q in range(6):
                    u, c = q // 3, q % 3
                    c0, cn = CHUNKS[c]
                    if c == 0:
                        pe.wait_ge(m_split, m * 2 + (u + 1))
                    if q < 4:
                        pe.wait_ge(m_mul, m * 6 + (q + 3))
                    high, low = hx_hi[c][:, :, :], hx_lo[:, :, c0:c0 + cn]
                    product(bank(q, cn), [(m_hi[u][:, k, :], high[:, k, :]) for k in range(KT)]
                            + [(m_hi[u][:, k, :], low[:, k, :]) for k in range(KT)]
                            + [(m_lo[u][:, k, :], high[:, k, :]) for k in range(KT)]).then_inc(m_gate, 1)
                for q in range(6):
                    u, c = q // 3, q % 3
                    c0, cn = CHUNKS[c]
                    if c == 0:
                        pe.wait_ge(m_w_loaded[u], m * 16 + 16)
                    if q >= 2:
                        pe.wait_ge(m_sig, m * 6 + (q - 1))
                    product(bank(BRANCH_BANKS[q], cn),
                            [(m_w[u][:, k, :], (onaT, ofT)[u][:, k, c0:c0 + cn]) for k in range(4)])\
                        .then_inc(m_branch, 1)

            def project(t, u, free, arriving=False):
                pe.wait_ge(o_tok, t + 1)
                if free is not None:
                    pe.wait_ge(o_x1, free)
                    pe.wait_ge(o_logc, free)
                for k in range(KT):
                    if arriving and k % 2 == 0:
                        pe.wait_ge(wout_loaded[k // 2], 16)
                    for half in range(2):
                        op = pe.matmul(bank(2 * u + half), m_tok[u][:, k, :],
                                       w_out_sb[:, k, BANK * half:BANK * half + BANK],
                                       start=k == 0, stop=k == KT - 1)
                op.then_inc(o_mm, 1)

            def route(t, u, free):
                pe.wait_ge(o_xn, t + 1)
                if free is not None:
                    pe.wait_ge(o_h2, free)
                for k in range(KT):
                    op = pe.transpose(ps[:, 2048 + 1024 * u + P * k:2048 + 1024 * u + P * k + P],
                                      xn[u][:, P * k:P * k + P], ident[:, :])
                op.then_inc(o_tr, 1)
                pe.wait_ge(o_h2, t + 1)
                product(bank(2 * u, P, slice(0, EXPERTS)), [(wr_sb[:, k, :], h2T[u][:, k, :]) for k in range(KT)])\
                    .then_inc(o_log, 1)

            pe.wait_ge(m_out, len(CHUNKS) * KT)
            project(0, 0, None, arriving=True)
            project(1, 1, None)
            route(0, 0, None)
            with pe.Fori(0, NT // 2 - 1) as i:
                project(i * 2 + 2, 0, i * 2 + 1)
                route(i * 2 + 1, 1, None)
                project(i * 2 + 3, 1, i * 2 + 2)
                route(i * 2 + 2, 0, i * 2 + 1)
            route(NT - 1, 1, NT - 2)

            pe.wait_ge(o_logc, NT)
            for t in range(NT):
                op = pe.transpose(bank(0, EXPERTS, first=EXPERTS * t), logT[:, P * t:P * t + P],
                                  ident[0:EXPERTS, 0:EXPERTS])
            op.then_inc(r_tr, 1)
            pe.wait_ge(r_dve, 6)
            for t in range(NT):
                op = pe.transpose(ps[0:EXPERTS, BANK + P * t:BANK + P * t + P], aff_tok[:, t, :], ident[:, :])
            op.then_inc(r_tr, 1)
            pe.wait_ge(r_exp, 2)
            for n, src in enumerate((top_v, top_f)):
                for k0, cap in ((0, CAP_P), (CAP_P, CAP_S)):
                    op = pe.transpose(bank(0, EXPERTS, slice(0, cap), 2 * n * EXPERTS + (EXPERTS if k0 else 0)),
                                      src[:, k0:k0 + cap], ident[0:EXPERTS, 0:EXPERTS])
            op.then_inc(r_tr, 1)

            def expert_transposes():
                for b, k0, kn in X_BANKS:
                    for k in range(k0, k0 + kn):
                        col = CAP * (k - k0)
                        pe.transpose(bank(b, P, first=col), xg_p[:, P * k:P * k + P], ident[:, :])
                        op = pe.transpose(bank(b, CAP_S, first=col + P), xg_s[:, P * k:P * k + P],
                                          ident[0:CAP_S, 0:CAP_S])
                op.then_inc(x_tr, 1)

            def split_product(out, n, v, cols, hl, b, part=None):
                part = part or range(n)
                for k in part:
                    pe.matmul(out, unit(w_hi, v)[:, k, cols], hl[:, k, :, :].rearrange("p a n -> p (a n)"),
                              start=k == 0, stop=False)
                for k in part:
                    op = pe.matmul(out[:, CAP:2 * CAP], unit(w_lo, v)[:, k, cols], b[:, k, :],
                                   start=False, stop=k == n - 1)
                return op

            def tile_of_gate_and_up(e, j):
                b = 2 * (j % 2)
                for n in range(2):
                    v = j // 2 * 2 + n
                    if j % 2 == 0:
                        wait_split(pe, e, v)
                    op = split_product(bank(b + n, 2 * CAP), KT, v, slice(P * (j % 2), P * (j % 2) + P), x_hl, x_b)
                op.then_inc(gu_ready, 1)

            pe.sem_inc(down_ready, KT)
            pe.wait_ge(rows_moved, 32)
            expert_transposes()
            pe.wait_ge(first_units, LEAD)
            pe.wait_ge(x_ready, 1)
            tile_of_gate_and_up(0, 0)
            with pe.Fori(0, EXPERTS) as e:
                for j in range(1, FT):
                    if j >= 2:
                        pe.wait_ge(gu_added, e * FT + (j - 1))
                    tile_of_gate_and_up(e, j)
                pe.wait_ge(gu_added, e * FT + (FT - 1))
                pe.wait_ge(y_ready, e * 4 + 1)
                pe.wait_ge(rows_moved, e * 64 + 64)
                expert_transposes()

                def back(d):
                    (p, q), col = Y_BANKS[d // 4], P * (d % 4)
                    pe.wait_ge(yT_ready, e * KT + (d + 1))
                    if d == 4:
                        pe.wait_ge(xf_ready, e + 2)
                    pe.transpose(bank(p, P, first=col), yT[d % 2][:, 0:P], ident[:, :])
                    pe.transpose(bank(q, P, slice(0, CAP_S), col), yT[d % 2][:, P:CAP], ident[:, :])\
                      .then_inc(y_tr, 1)

                for d in range(KT):
                    wait_split(pe, e, 16 + d)
                    if d >= 2:
                        pe.wait_ge(yT_ready, e * KT + (d - 1))
                    out = bank(4 + d % 2, 2 * CAP)
                    if d == 0:
                        for k0, k1 in ((0, FT - 2), (FT - 2, FT)):
                            pe.wait_ge(act_ready, e * 8 + k1 // 2)
                            op = split_product(out, FT, 16, slice(0, P), act_hl, act_b, range(k0, k1))
                    else:
                        op = split_product(out, FT, 16 + d, slice(0, P), act_hl, act_b)
                    op.then_inc(down_ready, 1)
                    if d >= 1:
                        back(d - 1)
                pe.wait_ge(x_ready, e + 2)
                pe.wait_ge(y_ready, e * 4 + 3)
                tile_of_gate_and_up(e + 1, 0)
                back(KT - 1)


def dft_tables():
    def angles(n):
        return 2.0 * np.pi * (np.outer(np.arange(n), np.arange(n)) % n) / n

    a = angles(FD)
    tables = [np.concatenate([np.cos(a), np.sin(a)], 1)]
    for n in (S_PROMPT, S_SAMPLE):
        norm = 1.0 / np.sqrt(n * FD)
        tables += [np.cos(angles(n)) * norm, -np.sin(angles(n)) * norm]
    return [t.astype(np.float32) for t in tables]


def window_mask():
    c = np.arange(GRID)[:, None]
    c0 = np.clip(c - KW // 2, 0, GRID - KW)
    k = np.arange(GRID)[None, :]
    one = np.where((k >= c0) & (k < c0 + KW), 0.0, MASKED).astype(np.float32)
    return np.concatenate([one, one], 0)


def kernel(x_prompt, x_sample, norm1_g, w_in, q_norm_g, k_norm_g, rpb, w_na_out, w_fourier, w_out,
           norm2_g, w_router, w_gate_e, w_up_e, w_down_e):
    import concourse.bacc as bacc
    from concourse.bass_utils import run_bass_kernel_spmd

    arrays = {"x": np.concatenate([np.asarray(x_prompt)[0], np.asarray(x_sample)[0]], 0)}
    for name, a in (("g1", norm1_g), ("w_in", w_in), ("q_g", q_norm_g), ("k_g", k_norm_g), ("rpb", rpb),
                    ("w_na", w_na_out), ("w_fo", w_fourier), ("w_out", w_out), ("g2", norm2_g),
                    ("w_r", w_router), ("w_g", w_gate_e), ("w_u", w_up_e), ("w_d", w_down_e)):
        arrays[name] = np.ascontiguousarray(np.asarray(a)[0])
    for name in ("g1", "g2"):
        arrays[name] = np.ascontiguousarray(arrays[name].reshape(KT, P).T)
    for name, a in zip(("dft_c", "pos_c", "pos_s", "spos_c", "spos_s"), dft_tables()):
        arrays[name] = a
    arrays["col_mask"] = window_mask()
    nc = bacc.Bacc("TRN2", target_bir_lowering=False, num_devices=1)
    arrays = {f"in_{k}": v for k, v in arrays.items()}
    args = [nc.dram_tensor(k, v.shape, mybir.dt.from_np(v.dtype), kind="ExternalInput").ap()
            for k, v in arrays.items()]
    y = nc.dram_tensor("y_out", (TOK, D), F32, kind="ExternalOutput").ap()
    build(nc, *args, y)
    r = run_bass_kernel_spmd(nc, [arrays], core_ids=[0])
    got = r.results[0]["y_out"]
    return got[None, :S_PROMPT], got[None, S_PROMPT:]
```

```python
from contextlib import ExitStack

import concourse.bass as bass
import concourse.mybir as mybir
import numpy as np

F32 = mybir.dt.float32
F32R = mybir.dt.float32r
BF16 = mybir.dt.bfloat16
U32 = mybir.dt.uint32
ALU = mybir.AluOpType
ACT = mybir.ActivationFunctionType
AX = mybir.AxisListType

P = 128
D = 1024
KT = D // P
S_PROMPT, S_SAMPLE = 1024, 256
TOK = S_PROMPT + S_SAMPLE
NT = TOK // P
PT_TILES = S_PROMPT // P
CHUNKS = [(0, 512), (512, 512), (1024, 256)]
BANK = 512
GRID = 64
HEADS, DH = 8, 64
NA = HEADS * DH
KH, KW = 8, 16
FG, FD = 4, 128
F_COL = 3 * NA
GA_COL = F_COL + FG * FD
GF_COL = GA_COL + D
IN_W = GF_COL + D
EXPERTS, FF = 16, 2048
FT = FF // P
CAP_P = 2 * S_PROMPT // EXPERTS
CAP_S = 2 * S_SAMPLE // EXPERTS
CAP = CAP_P + CAP_S
EPS = 1e-6
MASKED = -1e30
BIAS_ROWS = 14
INNER_ROWS = KH + 1
RPB_H, RPB_W = 2 * KH - 1, 2 * KW - 1
BRANCH_BANKS = (6, 7, 0, 1, 2, 3)
LISTS, HALF = 3, S_PROMPT // 2
LIST_TILES = [t for a in range(HALF // P) for t in range(a, NT, HALF // P)]
A_TILES = 5
A_SLOT = (0, 1, 0, 1, 2)
P_SLOTS = 3
SKEW = 2 * GRID - 1


CHUNKS_E, UNITS = 12, 24
RAW_SLOTS, UNIT_SLOTS, LEAD = 4, 6, 4


def place_of(v):
    return (2 * (v // 4) + v % 2, v // 2 % 2) if v < 16 else (8 + (v - 16) // 2, v % 2)


def ahead(step):
    return [2 * step + LEAD, 2 * step + LEAD + 1] if step < 8 else [step + 8 + LEAD]


POOLS = [v for v in range(UNITS) if v % 3 == 2]
DVES = [v for v in range(UNITS) if v % 3 != 2]


def attention_tiles():
    tiles = []
    for base, rows in ((0, S_PROMPT // GRID), (S_PROMPT, S_SAMPLE // GRID)):
        kh = min(KH, rows)
        for r in range(0, rows, 2):
            lo = min(max(r - kh // 2, 0), rows - kh)
            hi = min(max(r + 1 - kh // 2, 0), rows - kh) + kh
            tiles.append((base + lo * GRID, hi - lo, lo - r + KH - 2, hi - lo > kh))
    return tiles


TILES = attention_tiles()
X_BANKS = ((6, 0, 3), (7, 3, 3), (0, 6, 2))
Y_BANKS = ((1, 2), (6, 7))


def build(nc, x, g1, w_in, q_g, k_g, rpb, w_na, w_fo, w_out, g2, w_r, w_g, w_u, w_d,
          dft_c, pos_c, pos_s, spos_c, spos_s, col_mask, y):
    ctx = ExitStack()
    with ctx:
        def sem(name):
            return ctx.enter_context(nc.semaphore(name))

        skew = nc.dram_tensor("skew_dram", (HEADS * RPB_H, GRID, SKEW), F32, kind="Internal").ap()
        xn_dram = nc.dram_tensor("xn_dram", (TOK, D), F32, kind="Internal").ap()

        base = -(-nc.sbuf_base // 32) * 32
        cursor = [base]

        def region(nbytes):
            at = cursor[0]
            cursor[0] += -(-nbytes // 32) * 32
            return at

        def at(name, shape, offset, dt=F32):
            return nc.alloc_sbuf_tensor_at(name, shape, dt, offset=offset)

        def put(name, shape, dt=F32):
            return at(name, shape, region(4 * int(np.prod(shape[1:]))), dt)

        ident = put("ident", [P, P])
        early_at = region(0)
        head_ones = put("head_ones", [P, P])
        mask_sb = put("mask_sb", [P, GRID])
        rpb_pad = put("rpb_pad", [HEADS * RPB_H, SKEW])
        assert region(0) - early_at >= 8 * CAP
        g1_sb = put("g1_sb", [P, KT])
        g2_sb = put("g2_sb", [P, KT])
        qk_g = put("qk_g", [P, 2])
        eps = put("eps", [P, 1])
        wr_sb = put("wr_sb", [P, KT, EXPERTS])
        ss = put("ss", [P, A_TILES])
        lnv = put("lnv", [P, A_TILES])
        rstd = put("rstd", [P, A_TILES])
        row_max = put("row_max", [P, P_SLOTS])
        neg_max = put("neg_max", [P, P_SLOTS])
        row_sum = put("row_sum", [P, P_SLOTS])
        row_rec = put("row_rec", [P, P_SLOTS])
        gate_t = put("gate_t", [P, 2, EXPERTS + 1])
        idx_t = put("idx_t", [P, 2, EXPERTS + 1], U32)
        gate_now = put("gate_now", [P, 2])
        idx_gather = put("idx_gather", [P, 2], U32)
        idx_scatter = put("idx_scatter", [P, 2], U32)

        H0 = region(0)
        hT = put("hT", [P, KT, TOK])
        ofT = put("ofT", [P, FG, TOK])
        onaT = put("onaT", [P, NA // P, TOK])
        Z0 = cursor[0]
        Z = [Z0]

        def z(name, shape, dt=F32):
            t = at(name, shape, Z[0], dt)
            Z[0] += -(-(2 if dt == BF16 else 4) * int(np.prod(shape[1:])) // 32) * 32
            return t

        pos_c_sb = z("pos_c_sb", [P, PT_TILES, S_PROMPT])
        pos_s_sb = z("pos_s_sb", [P, PT_TILES, S_PROMPT])
        spos_c_sb = z("spos_c_sb", [P, NT - PT_TILES, S_SAMPLE])
        spos_s_sb = z("spos_s_sb", [P, NT - PT_TILES, S_SAMPLE])
        dft_sb = z("dft_sb", [P, 2 * FD])
        f_w = z("f_w", [P, KT, FD])
        fT = z("fT", [P, TOK])
        f_mix = z("f_mix", [P, NT, 2 * FD])
        clear_at = Z[0]
        bias_raw = z("bias_raw", [P, 2, BIAS_ROWS, GRID])
        h_raw = z("h_raw", [P, KT, P])
        free_at = Z[0]
        hx_hi = {c: z(f"hx_hi{c}", [P, KT, CHUNKS[c][1]], F32R) for c in (0, 2)}
        hx_lo = at("hx_lo", [P, KT, TOK], H0, F32R)
        assert Z[0] <= nc.sbuf_usable_end
        Z[0] = Z0
        x_in = [z(f"x_in{u}", [P, D]) for u in range(A_TILES)]
        xn_a = [z(f"xn_a{u}", [P, D]) for u in range(3)]
        junk_a = z("junk_a", [P, D])
        assert Z[0] <= Z0 + 8 * PT_TILES * S_PROMPT
        Z[0] = Z0
        qkvT = z("qkvT", [P, 3, TOK])
        v_tok = z("v_tok", [P, NT, P])
        bias_all = z("bias_all", [P, 2, BIAS_ROWS, GRID])
        bias_in = z("bias_in", [P, 2, INNER_ROWS, GRID])
        p_at = Z[0]
        p_sb = [z(f"p_sb{u}", [P, INNER_ROWS * GRID]) for u in range(P_SLOTS)]
        pT = [z(f"pT{u}", [P, 5, P]) for u in range(2)]
        sq = [at(f"sq{u}", [P, BANK], p_at + 4 * BANK * u) for u in range(2)]
        rinv = [z(f"rinv{u}", [P, BANK]) for u in range(2)]
        parts_at = Z[0]
        w_high = [z(f"w_high{n}", [P, KT, P], F32R) for n in range(3)]
        w_low = [z(f"w_low{n}", [P, KT, P], F32R) for n in range(3)]
        hx_hi[1] = z("hx_hi1", [P, KT, CHUNKS[1][1]], F32R)
        assert Z[0] <= clear_at
        m_raw = [at(f"m_raw{u}", [P, KT, P], parts_at + 4 * KT * P * (2 + 3 * u)) for u in range(2)]
        Z[0] = clear_at
        m_w = [z(f"m_w{u}", [P, 4, P]) for u in range(2)]
        gated = [z("gated0", [P, BANK])]
        sig1 = z("sig1", [P, TOK])
        assert Z[0] <= free_at
        Z[0] = Z0
        mT = z("mT", [P, KT, TOK])
        sig_at = Z[0]
        sig = [z("sig0", [P, TOK]), sig1]
        gated.append(z("gated1", [P, BANK]))
        assert Z[0] <= parts_at
        Z[0] = sig_at
        raw_bytes = 4 * KT * 512
        w_out_sb = at("w_out_sb", [P, KT, D], H0 + 2 * raw_bytes)
        w_out_lo = at("w_out_lo", [P, KT, D], H0 + 2 * raw_bytes, F32R)
        w_out_hi = z("w_out_hi", [P, KT, D], F32R)
        m_tok_lo = [at(f"m_tok_lo{u}", [P, KT, P], H0 + 4 * raw_bytes + 4 * KT * P * u, F32R) for u in range(2)]
        Z[0] = Z0 + 4 * (KT * TOK + KT * D)
        x_res = [z(f"x_res{u}", [P, D]) for u in range(2)]
        x1 = [z(f"x1_{u}", [P, D]) for u in range(2)]
        xn = [z(f"xn{u}", [P, D]) for u in range(2)]
        h2T = [z(f"h2T{u}", [P, KT, P]) for u in range(2)]
        r_at = Z[0]
        m_tok_hi = [z(f"m_tok_hi{u}", [P, KT, P], F32R) for u in range(2)]
        junk_o = z("junk_o", [P, D])
        log_at = Z[0]
        logT = z("logT", [EXPERTS, TOK])
        assert Z[0] <= nc.sbuf_usable_end
        Z[0] = r_at
        log_tok = z("log_tok", [P, NT, EXPERTS])
        aff_tok = z("aff_tok", [P, NT, EXPERTS])
        r_max = z("r_max", [P, NT])
        r_sum = z("r_sum", [P, NT])
        aff = z("aff", [LISTS * EXPERTS, HALF])
        top_v = z("top_v", [LISTS * EXPERTS, CAP_P])
        top_i = z("top_i", [LISTS * EXPERTS, CAP_P], U32)
        top_f = z("top_f", [LISTS * EXPERTS, CAP_P])
        anti = z("anti", [P, P])
        half_2 = z("half_2", [P, 2, EXPERTS])
        turned = z("turned", [P, 2, EXPERTS])
        from_1 = z("from_1", [P, EXPERTS])
        sought = z("sought", [P, 2, EXPERTS])
        assert Z[0] <= log_at
        Z[0] = H0
        raw = [z(f"raw{s}", [P, KT * 512]) for s in range(RAW_SLOTS)]
        xg_p = z("xg_p", [P, D])
        xg_s = z("xg_s", [CAP_S, D])
        ye_p = z("ye_p", [P, D])
        ye_s = z("ye_s", [CAP_S, D])
        assert Z[0] <= Z0
        w_hi = [z(f"w_hi{s}", [P, KT * 256], F32R) for s in range(UNIT_SLOTS)]
        w_lo = [z(f"w_lo{s}", [P, KT * 256], BF16) for s in range(UNIT_SLOTS)]
        assert Z[0] <= Z0 + 4 * (KT * TOK + KT * D)
        act_hl = z("act_hl", [P, FT, 2, CAP], F32R)
        act_b = z("act_b", [P, FT, CAP], BF16)
        x_hl = z("x_hl", [P, KT, 2, CAP], F32R)
        x_b = z("x_b", [P, KT, CAP], BF16)
        x_f = z("x_f", [P, KT, CAP])
        act_f = [z(f"act_f{u}", [P, 2, CAP]) for u in range(2)]
        gu = [z(f"gu{u}", [P, 2, CAP]) for u in range(2)]
        lows = [z("lows0", [P, 2, CAP])]
        lows_at = Z[0]
        lows.append(z("lows1", [P, 2, CAP]))
        y_low = [at(f"y_low{u}", [P, CAP], lows_at + 4 * CAP * u) for u in range(2)]
        yT = [at(f"yT{u}", [P, CAP], early_at + 4 * CAP * u) for u in range(2)]
        silu = [z(f"silu{u}", [P, CAP]) for u in range(2)]
        assert Z[0] <= nc.sbuf_usable_end

        ps = ctx.enter_context(nc.psum_tensor("ps", [P, 8 * BANK], F32))

        def bank(b, n=BANK, parts=slice(0, P), first=0):
            return ps[parts, b * BANK + first:b * BANK + first + n]

        def gate_up(b):
            return ps[:, b * BANK:(b + 2) * BANK].rearrange("p (g n) -> p g n", n=BANK)

        ident_ready = sem("ident_ready")
        ones_cleared = sem("ones_cleared")
        CONSTS = 6
        const_ready = sem("const_ready")
        small_loaded = sem("small_loaded")
        pad_ready = sem("pad_ready")
        pad_loaded = sem("pad_loaded")
        skew_stored = sem("skew_stored")
        mask_loaded = sem("mask_loaded")
        a_loaded = [sem(f"a_loaded{u}") for u in range(A_TILES)]
        a_stat = sem("a_stat")
        a_norm = sem("a_norm")
        a_tr = sem("a_tr")
        a_out = sem("a_out")
        dft_loaded = sem("dft_loaded")
        f_tables = sem("f_tables")
        f_loaded = sem("f_loaded")
        f_proj = sem("f_proj")
        f_copied = sem("f_copied")
        f_chan = sem("f_chan")
        f_mixed = sem("f_mixed")
        f_pos = sem("f_pos")
        f_out = sem("f_out")
        h_loaded = sem("h_loaded")
        b_loaded = sem("b_loaded")
        b_step = sem("b_step")
        h_proj = sem("h_proj")
        h_sq = sem("h_sq")
        h_ss = sem("h_ss")
        h_ln = sem("h_ln")
        h_rinv = sem("h_rinv")
        h_qk = sem("h_qk")
        h_vT = sem("h_vT")
        h_vtr = sem("h_vtr")
        h_v = sem("h_v")
        s_ready = sem("s_ready")
        s_added = sem("s_added")
        s_max = sem("s_max")
        p_exp = sem("p_exp")
        p_rec = sem("p_rec")
        p_ready = sem("p_ready")
        p_tr = sem("p_tr")
        p_copied = sem("p_copied")
        pv_done = sem("pv_done")
        o_out = sem("o_out")
        m_raw_loaded = [sem(f"m_raw_loaded{u}") for u in range(2)]
        m_w_loaded = [sem(f"m_w_loaded{u}") for u in range(2)]
        hx_high = sem("hx_high")
        hx_ready = sem("hx_ready")
        hx1_ready = sem("hx1_ready")
        h_high = sem("h_high")
        h_split = sem("h_split")
        m_high = sem("m_high")
        m_split = sem("m_split")
        m_gate = sem("m_gate")
        m_branch = sem("m_branch")
        m_sig = sem("m_sig")
        m_mul = sem("m_mul")
        m_out = sem("m_out")
        wout_high = sem("wout_high")
        wout_split = sem("wout_split")
        o_high = sem("o_high")
        wout_loaded = [sem(f"wout_loaded{n}") for n in range(KT)]
        r_loaded = [sem(f"r_loaded{u}") for u in range(2)]
        o_tok = sem("o_tok")
        o_mm = sem("o_mm")
        o_x1 = sem("o_x1")
        o_stat = sem("o_stat")
        o_xn = sem("o_xn")
        o_tr = sem("o_tr")
        o_h2 = sem("o_h2")
        o_log = sem("o_log")
        o_logc = sem("o_logc")
        x1_stored = [sem(f"x1_stored{u}") for u in range(2)]
        xn_stored = [sem(f"xn_stored{u}") for u in range(2)]
        r_tr = sem("r_tr")
        r_dve = sem("r_dve")
        r_exp = sem("r_exp")
        raw_loaded = [sem(f"raw_loaded{s}") for s in range(RAW_SLOTS)]
        hi_ready = sem("hi_ready")
        lo_dve = sem("lo_dve")
        lo_pool = sem("lo_pool")
        first_units = sem("first_units")
        cols_ready = sem("cols_ready")
        anti_ready = sem("anti_ready")
        r_half = sem("r_half")
        rows_moved = sem("rows_moved")
        x_tr = sem("x_tr")
        xf_ready = sem("xf_ready")
        x_hi_ready = sem("x_hi_ready")
        x_ready = sem("x_ready")
        gu_ready = sem("gu_ready")
        low_ready = sem("low_ready")
        gu_added = sem("gu_added")
        silu_ready = sem("silu_ready")
        act_f_ready = sem("act_f_ready")
        act_hi_ready = sem("act_hi_ready")
        act_ready = sem("act_ready")
        down_ready = sem("down_ready")
        y_low_ready = sem("y_low_ready")
        yT_ready = sem("yT_ready")
        y_tr = sem("y_tr")
        y_ready = sem("y_ready")

        pool_passed, dve_passed, sp_passed = sem("pool_passed"), sem("dve_passed"), sem("sp_passed")

        def apart(engine, passed):
            engine.sem_inc(passed, 1)

        def wait_consumed(engine, e, v):
            if 0 <= v < 16:
                engine.wait_ge(gu_ready, e * FT + (v // 2 * 2 + 2))
            else:
                engine.wait_ge(down_ready, e * KT + (v % UNITS - 16 + 1 + (KT if v >= 0 else 0)))

        def wait_split(engine, e, v):
            if v in POOLS:
                engine.wait_ge(lo_pool, e * len(POOLS) + (POOLS.index(v) + 1))
            else:
                engine.wait_ge(lo_dve, e * len(DVES) + (DVES.index(v) + 1))

        def raw_half(v):
            c, half = place_of(v)
            n = 256 if v < 16 else 128
            return raw[c % RAW_SLOTS][:, :].rearrange("p (k n) -> p k n", n=2 * n)[:, :, n * half:n * half + n]

        def unit(ring, v):
            return ring[v % UNIT_SLOTS][:, :].rearrange("p (k n) -> p k n", n=256 if v < 16 else 128)

        def low_part(engine, e, v, signal):
            engine.wait_ge(hi_ready, e * UNITS + (v + 1))
            v %= UNITS
            engine.tensor_tensor(unit(w_lo, v), raw_half(v), unit(w_hi, v).bitcast(F32), ALU.subtract)\
                  .then_inc(signal, 1)

        block = ctx.enter_context(nc.Block())

        @block.sync
        def _(sp):
            ts = bass.ts
            for u in range(2):
                sp.dma_start(x_in[u][:, :], x[u * P:u * P + P, :]).then_inc(a_loaded[u], 16)
            sp.dma_start(g1_sb[:, :], g1).then_inc(small_loaded, 16)
            sp.dma_start(g2_sb[:, :], g2).then_inc(small_loaded, 16)
            for n, g in enumerate((q_g, k_g)):
                for half in range(2):
                    sp.dma_start(qk_g[DH * half:DH * half + DH, n:n + 1], g.rearrange("(p o) -> p o", o=1))\
                      .then_inc(small_loaded, 16)
            sp.dma_start(wr_sb[:, :, :], w_r.rearrange("(k p) e -> p k e", p=P)).then_inc(small_loaded, 16)
            for u in range(2, A_TILES):
                sp.dma_start(x_in[u][:, :], x[u * P:u * P + P, :]).then_inc(a_loaded[u], 16)
            for u in range(A_TILES):
                sp.wait_ge(a_norm, u + 1)
                sp.dma_start(x_in[u][:, :], x[(A_TILES + u) * P:(A_TILES + u + 1) * P, :])\
                  .then_inc(a_loaded[u], 16)
            sp.dma_start(f_w[:, :, :], w_in[:, F_COL:F_COL + FD].rearrange("(k p) n -> p k n", p=P))\
              .then_inc(f_loaded, 16)
            sp.dma_start(dft_sb[:, :], dft_c).then_inc(dft_loaded, 16)
            sp.wait_ge(a_norm, NT)
            sp.wait_ge(a_tr, NT)
            sp.dma_start(pos_c_sb[:, :, :], pos_c.rearrange("(k p) n -> p k n", p=P)).then_inc(f_tables, 16)
            sp.dma_start(pos_s_sb[:, :, :], pos_s.rearrange("(k p) n -> p k n", p=P)).then_inc(f_tables, 16)
            sp.dma_start(spos_c_sb[:, :, :], spos_c.rearrange("(k p) n -> p k n", p=P)).then_inc(f_tables, 16)
            sp.dma_start(spos_s_sb[:, :, :], spos_s.rearrange("(k p) n -> p k n", p=P)).then_inc(f_tables, 16)
            with sp.Fori(0, FG - 1) as g:
                sp.wait_ge(f_proj, g * 3 + 3)
                sp.dma_start(f_w[:, :, :], w_in[:, bass.ds(g * FD + (F_COL + FD), FD)]
                             .rearrange("(k p) n -> p k n", p=P)).then_inc(f_loaded, 16)

            def head_load(hp, n):
                sp.dma_start(h_raw[:, :, :], w_in[:, bass.ds(hp * P + n * NA, P)]
                             .rearrange("(k p) n -> p k n", p=P)).then_inc(h_loaded, 16)

            def bias_loads(hp):
                for hh in range(2):
                    for ri in range(2):
                        rows = skew[bass.ds((hp * 2 + hh) * RPB_H + (1 - ri), BIAS_ROWS), :, :]
                        src = bass.AP(rows.tensor, rows.offset + (GRID - 1),
                                      [[SKEW - 1, GRID], [GRID * SKEW, BIAS_ROWS], [1, GRID]])
                        sp.dma_start(bias_raw[GRID * ri:GRID * ri + GRID, hh, :, :], src).then_inc(b_loaded, 16)

            head_load(0, 0)
            sp.wait_ge(skew_stored, 16)
            bias_loads(0)
            for n in range(1, 3):
                sp.wait_ge(h_split, n)
                head_load(0, n)
            with sp.Fori(1, HEADS // 2) as hp:
                for n in range(3):
                    sp.wait_ge(h_split, hp * 3 + n)
                    apart(sp, sp_passed)
                    head_load(hp, n)
                sp.wait_ge(b_step, hp * 8 - 6)
                bias_loads(hp)

            def load_gate(m, u):
                sp.dma_start(m_raw[u][:, :, :], w_in[:, bass.ds(m * P + (GA_COL, GF_COL)[u], P)]
                             .rearrange("(k p) n -> p k n", p=P)).then_inc(m_raw_loaded[u], 16)

            def load_branch(m, u):
                sp.dma_start(m_w[u][:, :, :], (w_na, w_fo)[u][:, bass.ds(m * P, P)]
                             .rearrange("(k p) n -> p k n", p=P)).then_inc(m_w_loaded[u], 16)

            sp.wait_ge(h_proj, HEADS // 2 * 9)
            sp.wait_ge(b_step, HEADS // 2 * 8)
            for u in range(2):
                load_gate(0, u)
                load_branch(0, u)
            with sp.Fori(0, KT - 1) as m:
                for u in range(2):
                    sp.wait_ge(m_split, m * 2 + (u + 1))
                    apart(sp, sp_passed)
                    load_gate(m + 1, u)
                for u in range(2):
                    sp.wait_ge(m_branch, m * 6 + (3 * u + 3))
                    apart(sp, sp_passed)
                    load_branch(m + 1, u)

            def expert_load(e, c):
                s = c % RAW_SLOTS
                n = 512 if c < 8 else 256
                w, col = ((w_g, w_u)[c % 2], c // 2 * n) if c < 8 else (w_d, (c - 8) * n)
                sp.dma_start(raw[s][:, :].rearrange("p (k n) -> p k n", n=n),
                             w[bass.ds(e, 1), :, col:col + n].rearrange("a (k p) n -> p (a k) n", p=P))\
                  .then_inc(raw_loaded[s], 16)

            sp.wait_ge(m_out, len(CHUNKS) * KT)
            for n in range(KT):
                sp.dma_start(w_out_sb[:, n, :], w_out[P * n:P * n + P, :]).then_inc(wout_loaded[n], 16)
            for u in range(2):
                sp.dma_start(x_res[u][:, :], x[u * P:u * P + P, :]).then_inc(r_loaded[u], 16)
            for c in range(2):
                expert_load(0, c)

            def store_x1(t, u, n):
                sp.wait_ge(o_x1, t + 1)
                sp.dma_start(y[ts(t, P), :], x1[u][:, :]).then_inc(x1_stored[u], 16)

            def store_xn(t, u, n):
                sp.wait_ge(o_xn, t + 1)
                sp.dma_start(xn_dram[ts(t, P), :], xn[u][:, :]).then_inc(xn_stored[u], 16)

            with sp.Fori(0, NT // 2 - 1) as i:
                for u in range(2):
                    store_x1(i * 2 + u, u, i)
                    sp.dma_start(x_res[u][:, :], x[ts(i * 2 + (u + 2), P), :]).then_inc(r_loaded[u], 16)
                    store_xn(i * 2 + u, u, i)
            for u in range(2):
                store_x1(NT - 2 + u, u, 0)
                store_xn(NT - 2 + u, u, 0)
            sp.wait_ge(o_mm, NT)
            for c in range(2, RAW_SLOTS):
                expert_load(0, c)

            def wait_chunk_split(e, c):
                for v in range(UNITS):
                    if place_of(v)[0] == c:
                        wait_split(sp, e, v)
                        apart(sp, sp_passed)

            sp.wait_ge(first_units, LEAD)
            with sp.Fori(0, EXPERTS - 1) as e:
                for c in range(CHUNKS_E):
                    wait_chunk_split(e, c)
                    n = c + RAW_SLOTS
                    expert_load(e + n // CHUNKS_E, n % CHUNKS_E)
            for c in range(CHUNKS_E - RAW_SLOTS):
                wait_chunk_split(EXPERTS - 1, c)
                expert_load(EXPERTS - 1, c + RAW_SLOTS)
            for c in range(2):
                sp.wait_ge(raw_loaded[c], 16 * 3 * EXPERTS)
                sp.sem_inc(raw_loaded[c], 16)
            for u in range(2):
                sp.wait_ge(x1_stored[u], 16 * (NT // 2))
                sp.wait_ge(xn_stored[u], 16 * (NT // 2))
            sp.wait_ge(rows_moved, 64 * EXPERTS + 32)

        @block.gpsimd
        def _(pool):
            pool.memset(ident[:, :], 0.0).then_inc(ident_ready, 1)
            pool.memset(eps[:, :], EPS).then_inc(const_ready, 1)
            pool.wait_ge(ident_ready, 1)
            pool.affine_select(out=ident[:, :], in_=ident[:, :], compare_op=ALU.not_equal, fill=1.0,
                               base=0, pattern=[[-1, P]], channel_multiplier=1).then_inc(ident_ready, 1)
            pool.memset(idx_t[:, :, :], 0).then_inc(const_ready, 1)
            pool.memset(gate_t[:, :, :], 0.0).then_inc(const_ready, 1)
            pool.memset(rpb_pad[:, :], 0.0).then_inc(pad_ready, 1)
            pool.wait_ge(pad_ready, 1)
            pool.dma_start(rpb_pad[:, GRID - KW:GRID - KW + RPB_W], rpb.rearrange("h j x -> (h j) x"))\
                .then_inc(pad_loaded, 16)
            pool.wait_ge(pad_loaded, 16)
            pool.wait_ge(f_tables, 16 * 4)
            pool.dma_start(skew, rpb_pad[:, :].rearrange("q (o x) -> q o x", o=1)
                           .broadcast_to([HEADS * RPB_H, GRID, SKEW])).then_inc(skew_stored, 16)
            pool.dma_start(mask_sb[:, :], col_mask).then_inc(mask_loaded, 16)
            pool.wait_ge(mask_loaded, 16)
            for n, c in enumerate((0, 2)):
                c0, cn = CHUNKS[c]
                pool.wait_ge(hx_high, n + 1)
                pool.tensor_tensor(hx_lo[:, :, c0:c0 + cn], hT[:, :, c0:c0 + cn], hx_hi[c][:, :, :].bitcast(F32),
                                   ALU.subtract).then_inc(hx_ready, 1)
                pool.wait_ge(hx_ready, n + 1)
            pool.wait_ge(f_out, 3 * FG)
            mask_b = mask_sb[:, :].rearrange("p (o x) -> p o x", o=1)
            def weight_parts(hp, n):
                pool.wait_ge(h_loaded, hp * 48 + (16 * n + 16))
                apart(pool, pool_passed)
                pool.tensor_copy(w_high[n][:, :, :], h_raw[:, :, :]).then_inc(h_high, 1)
                pool.wait_ge(h_high, hp * 3 + (n + 1))
                pool.tensor_tensor(w_low[n][:, :, :], h_raw[:, :, :], w_high[n][:, :, :].bitcast(F32),
                                   ALU.subtract).then_inc(h_split, 1)
                pool.wait_ge(h_split, hp * 3 + (n + 1))
                apart(pool, pool_passed)

            def mask_bias(hp):
                pool.wait_ge(b_loaded, hp * 64 + 64)
                pool.wait_ge(o_out, hp * NT + 1)
                for hh in range(2):
                    pool.tensor_tensor(bias_all[:, hh, :, :], bias_raw[:, hh, :, :],
                                       mask_b.broadcast_to([P, BIAS_ROWS, GRID]), ALU.add).then_inc(b_step, 1)
                pool.wait_ge(b_step, hp * 8 + 2)
                apart(pool, pool_passed)
                for hh in range(2):
                    first = KH - 2 - KH // 2
                    pool.tensor_copy(bias_in[:, hh, :, :], bias_all[:, hh, first:first + INNER_ROWS, :])\
                        .then_inc(b_step, 1)
                pool.wait_ge(b_step, hp * 8 + 4)
                apart(pool, pool_passed)
                for hh in range(2):
                    pool.memset(bias_in[0:GRID, hh, INNER_ROWS - 1, :], MASKED).then_inc(b_step, 1)
                    pool.memset(bias_in[GRID:P, hh, 0, :], MASKED).then_inc(b_step, 1)

            for n in range(3):
                weight_parts(0, n)
            with pool.Fori(0, HEADS // 2 - 1) as hp:
                mask_bias(hp)
                pool.wait_ge(b_step, hp * 8 + 8)
                apart(pool, pool_passed)
                for n in range(3):
                    pool.wait_ge(h_proj, hp * 9 + (3 * n + 3))
                    apart(pool, pool_passed)
                    weight_parts(hp + 1, n)
            mask_bias(HEADS // 2 - 1)
            pool.wait_ge(b_step, HEADS // 2 * 8)
            pool.wait_ge(h_proj, HEADS // 2 * 9)

            def gate_parts(m, u):
                pool.wait_ge(m_raw_loaded[u], m * 16 + 16)
                apart(pool, pool_passed)
                pool.wait_ge(m_gate, m * 6 + (3 * u + 3))
                apart(pool, pool_passed)
                pool.tensor_copy(w_high[u][:, :, :], m_raw[u][:, :, :]).then_inc(m_high, 1)
                pool.wait_ge(m_high, m * 2 + (u + 1))
                pool.tensor_tensor(w_low[u][:, :, :], m_raw[u][:, :, :], w_high[u][:, :, :].bitcast(F32),
                                   ALU.subtract).then_inc(m_split, 1)
                pool.wait_ge(m_split, m * 2 + (u + 1))
                apart(pool, pool_passed)

            with pool.Fori(0, KT) as m:
                for u in range(2):
                    gate_parts(m, u)
            pool.wait_ge(o_mm, NT)
            pool.memset(anti[:, :], 0.0).then_inc(anti_ready, 1)
            pool.wait_ge(anti_ready, 1)
            pool.affine_select(out=anti[:, :], in_=anti[:, :], compare_op=ALU.not_equal, fill=1.0,
                               base=1 - P, pattern=[[1, P]], channel_multiplier=1).then_inc(anti_ready, 1)
            pool.wait_ge(anti_ready, 2)
            pool.sem_inc(lo_pool, sum(v in POOLS for v in range(LEAD)))
            for v in range(LEAD):
                low_part(pool, 0, v, first_units)
            pool.wait_ge(cols_ready, 1)
            for u in range(2):
                pool.wait_ge(xn_stored[u], 16 * (NT // 2))
                pool.wait_ge(x1_stored[u], 16 * (NT // 2))
            xg_count = sem("gather_cols")
            sc_count = sem("scatter_cols")

            def gather(n):
                pool.tensor_copy(idx_gather[:, :], idx_t[:, :, bass.ds(n, 1)].rearrange("p a b -> p (a b)"))\
                    .then_inc(xg_count, 1)
                pool.wait_ge(xg_count, n + 1)
                apart(pool, pool_passed)
                pool.indirect_dma_start(xg_p[:, :], None, xn_dram,
                                        bass.IndirectOffsetOnAxis(idx_gather[:, 0:1], 0)).then_inc(rows_moved, 16)
                pool.indirect_dma_start(xg_s[:, :], None, xn_dram,
                                        bass.IndirectOffsetOnAxis(idx_gather[0:CAP_S, 1:2], 0))\
                    .then_inc(rows_moved, 16)

            def lows(e, step):
                for v in ahead(step):
                    if v % UNITS in POOLS:
                        low_part(pool, e, v, lo_pool)

            gather(0)
            with pool.Fori(0, EXPERTS) as e:
                lows(e, 0)
                pool.wait_ge(x_tr, e + 1)
                gather(e + 1)
                for step in range(1, 4):
                    lows(e, step)
                pool.wait_ge(rows_moved, e * 64 + 64)
                pool.tensor_copy(idx_scatter[:, :], idx_t[:, :, bass.ds(e, 1)].rearrange("p a b -> p (a b)"))\
                    .then_inc(sc_count, 1)
                pool.tensor_copy(gate_now[:, :], gate_t[:, :, bass.ds(e, 1)].rearrange("p a b -> p (a b)"))\
                    .then_inc(sc_count, 1)
                pool.wait_ge(sc_count, e * 2 + 2)
                pool.sem_inc(cols_ready, 1)
                for step in range(4, 16):
                    lows(e, step)
                pool.wait_ge(y_ready, e * 4 + 5)
                apart(pool, pool_passed)
                pool.indirect_dma_start(y, bass.IndirectOffsetOnAxis(idx_scatter[:, 0:1], 0), ye_p[:, :], None,
                                        compute_op=ALU.add).then_inc(rows_moved, 16)
                pool.indirect_dma_start(y, bass.IndirectOffsetOnAxis(idx_scatter[0:CAP_S, 1:2], 0),
                                        ye_s[:, :], None, compute_op=ALU.add).then_inc(rows_moved, 16)
            pool.wait_ge(rows_moved, 64 * EXPERTS + 32)

        @block.scalar
        def _(act):
            act.preload_act_table_set("natural_log_exp_and_others")
            act.wait_ge(const_ready, CONSTS)

            def inv_rms(step, n, src, u, length):
                act.wait_ge(step, n + 1)
                act.activation(lnv[:, u:u + 1], src, ACT.Ln, bias=eps[:, 0:1], scale=1.0 / length)\
                   .then_inc(step, 1)
                act.wait_ge(step, n + 2)
                act.activation(rstd[:, u:u + 1], lnv[:, u:u + 1], ACT.Exp, scale=-0.5).then_inc(step, 1)

            with act.Fori(0, NT // A_TILES) as i:
                for u in range(A_TILES):
                    n = (i * A_TILES + u) * 3
                    act.wait_ge(a_loaded[u], i * 16 + 16)
                    act.activation(junk_a[:, :], x_in[u][:, :], ACT.Square, accum_out=ss[:, u:u + 1])\
                       .then_inc(a_stat, 1)
                    inv_rms(a_stat, n, ss[:, u:u + 1], u, D)
            with act.Fori(0, FG) as g:
                for c, (c0, cn) in enumerate(CHUNKS):
                    act.wait_ge(f_proj, g * 3 + (c + 1))
                    act.activation(fT[:, c0:c0 + cn], bank(c, cn), ACT.Copy).then_inc(f_copied, 1)
            for c in (0, 2, 1):
                c0, cn = CHUNKS[c]
                if c == 1:
                    act.wait_ge(f_out, 3 * FG)
                act.activation(hx_hi[c][:, :, :], hT[:, :, c0:c0 + cn], ACT.Copy).then_inc(hx_high, 1)
            with act.Fori(0, HEADS // 2) as hp:
                def rinv_of(j):
                    cn = CHUNKS[j % 3][1]
                    act.wait_ge(h_ss, hp * 6 + (j + 1))
                    if j >= 2:
                        act.wait_ge(h_qk, hp * 6 + (j - 1))
                    act.activation(rinv[j % 2][:, 0:cn], bank(3 + j % 2, cn), ACT.Ln, bias=eps[:, 0:1],
                                   scale=1.0 / DH).then_inc(h_ln, 1)
                    act.wait_ge(h_ln, hp * 6 + (j + 1))
                    act.activation(rinv[j % 2][:, 0:cn], rinv[j % 2][:, 0:cn], ACT.Exp, scale=-0.5)\
                       .then_inc(h_rinv, 1)

                for j in range(9):
                    c0, cn = CHUNKS[j % 3]
                    act.wait_ge(h_proj, hp * 9 + (j + 1))
                    if j < 6:
                        if j >= 2:
                            act.wait_ge(h_ss, hp * 6 + (j - 1))
                        act.activation(sq[j % 2][:, 0:cn], bank(j % 3, cn), ACT.Square).then_inc(h_sq, 1)
                    else:
                        act.activation(qkvT[:, 2, c0:c0 + cn], bank(j % 3, cn), ACT.Copy).then_inc(h_vT, 1)
                    if 1 <= j < 7:
                        rinv_of(j - 1)

                def exponent(j):
                    nk = TILES[j // 2][1] * GRID
                    act.wait_ge(s_max, hp * 20 + (j + 1))
                    u = j % P_SLOTS
                    act.activation(p_sb[u][:, 0:nk], p_sb[u][:, 0:nk], ACT.Exp,
                                   bias=neg_max[:, u:u + 1], accum_out=row_sum[:, u:u + 1])\
                       .then_inc(p_exp, 1)

                exponent(0)
                exponent(1)
                for j in range(20):
                    if j < 18:
                        exponent(j + 2)
                    nk = TILES[j // 2][1] * GRID
                    full = min(nk // P, 4)
                    act.wait_ge(p_tr, hp * 20 + (j + 1))
                    if j >= 2:
                        act.wait_ge(pv_done, hp * 20 + (j - 1))
                    if nk > 4 * P:
                        act.activation(pT[j % 2][0:GRID, 4, :], bank(3, P, slice(0, GRID)), ACT.Copy)
                    act.activation(pT[j % 2][:, 0:full, :], bank(2, full * P).rearrange("p (k n) -> p k n", n=P),
                                   ACT.Copy).then_inc(p_copied, 1)
            act.preload_act_table(ACT.Sigmoid)
            with act.Fori(0, KT) as m:
                for u in range(2):
                    for c, (c0, cn) in enumerate(CHUNKS):
                        q = 3 * u + c
                        act.wait_ge(m_mul, m * 6 + (q + 1))
                        act.wait_ge(m_gate, m * 6 + (q + 7))
                        act.activation(sig[u][:, c0:c0 + cn], bank(q, cn), ACT.Sigmoid).then_inc(m_sig, 1)
            act.preload_act_table_set("natural_log_exp_and_others")
            for n in range(KT):
                act.wait_ge(wout_loaded[n], 16)
                act.activation(w_out_hi[:, n, :], w_out_sb[:, n, :], ACT.Copy)\
                   .then_inc(wout_high, 1)
            with act.Fori(0, NT // 2) as i:
                for u in range(2):
                    n = (i * 2 + u) * 3
                    act.wait_ge(o_x1, i * 2 + (u + 1))
                    act.activation(junk_o[:, :], x1[u][:, :], ACT.Square, accum_out=ss[:, u:u + 1])\
                       .then_inc(o_stat, 1)
                    inv_rms(o_stat, n, ss[:, u:u + 1], u, D)
            act.wait_ge(r_dve, 3)
            act.activation(aff_tok[:, :, :], log_tok[:, :, :], ACT.Exp).then_inc(r_exp, 1)
            act.preload_act_table(ACT.Silu)

            def high_part(e, v, first=False):
                n, w = v // UNITS, v % UNITS
                c = place_of(w)[0]
                act.wait_ge(raw_loaded[c % RAW_SLOTS], e * 48 + 16 * (3 * n + c // RAW_SLOTS + 1))
                if not first:
                    wait_consumed(act, e, v - UNIT_SLOTS)
                act.activation(unit(w_hi, w), raw_half(w), ACT.Copy).then_inc(hi_ready, 1)

            act.wait_ge(o_mm, NT)
            for v in range(LEAD):
                high_part(0, v, first=True)

            def token_high(n):
                act.wait_ge(xf_ready, n + 1)
                act.activation(x_hl[:, :, 0, :], x_f[:, :, :], ACT.Copy).then_inc(x_hi_ready, 1)

            token_high(0)
            with act.Fori(0, EXPERTS) as e:
                def low_sums(j):
                    b = 2 * (j % 2)
                    act.wait_ge(gu_ready, e * FT + (j + 1))
                    if j >= 2:
                        act.wait_ge(gu_added, e * FT + (j - 1))
                    act.activation(lows[j % 2][:, :, :], gate_up(b)[:, :, CAP:2 * CAP], ACT.Copy)\
                       .then_inc(low_ready, 1)

                def gate(j):
                    act.wait_ge(gu_added, e * FT + (j + 1))
                    if j >= 2:
                        act.wait_ge(act_f_ready, e * FT + (j - 1))
                    act.activation(silu[j % 2][:, :], gu[j % 2][:, 0, :], ACT.Silu).then_inc(silu_ready, 1)

                def act_high(pair):
                    act.wait_ge(act_f_ready, e * FT + (2 * pair + 2))
                    act.activation(act_hl[:, 2 * pair:2 * pair + 2, 0, :], act_f[pair % 2][:, :, :], ACT.Copy)\
                       .then_inc(act_hi_ready, 1)

                def y_lows(d):
                    act.wait_ge(down_ready, e * KT + (KT + d + 1))
                    if d >= 2:
                        act.wait_ge(yT_ready, e * KT + (d - 1))
                    act.activation(y_low[d % 2][:, :], bank(4 + d % 2, CAP, first=CAP), ACT.Copy)\
                       .then_inc(y_low_ready, 1)

                for step in range(8):
                    if step:
                        low_sums(2 * step - 1)
                    high_part(e, ahead(step)[0])
                    if step:
                        gate(2 * step - 1)
                    low_sums(2 * step)
                    high_part(e, ahead(step)[1])
                    if step:
                        act_high(step - 1)
                    gate(2 * step)
                low_sums(FT - 1)
                gate(FT - 1)
                act_high(7)
                for d in range(KT):
                    high_part(e, ahead(8 + d)[0])
                    y_lows(d)
                    if d == 1:
                        token_high(e + 1)

        @block.vector
        def _(dve):
            dve.sem_inc(o_out, 1)
            dve.sem_inc(m_mul, 6)
            dve.sem_inc(lo_dve, sum(v in DVES for v in range(LEAD)))
            dve.sem_inc(y_ready, 1)

            def times_gain(out, src, gain, inner):
                return dve.tensor_tensor(out, src, gain.rearrange("p (k o) -> p k o", o=1)
                                         .broadcast_to([P, gain.shape[1], inner]), ALU.mult)

            dve.memset(head_ones[:, :], 0.0).then_inc(ones_cleared, 1)
            for half in range(2):
                a = DH * half
                dve.wait_ge(ones_cleared, 1)
                dve.memset(head_ones[a:a + DH, a:a + DH], 1.0).then_inc(const_ready, 1)
            dve.wait_ge(small_loaded, 16 * 7)
            dve.tensor_scalar(qk_g[:, 0:1], qk_g[:, 0:1], DH ** -0.5, None, ALU.mult).then_inc(const_ready, 1)
            with dve.Fori(0, NT // A_TILES) as i:
                def norm(u):
                    dve.wait_ge(a_stat, i * (3 * A_TILES) + (3 * u + 3))
                    dve.tensor_scalar(xn_a[A_SLOT[u]][:, :], x_in[u][:, :], rstd[:, u:u + 1], None, ALU.mult)\
                       .then_inc(a_norm, 1)

                def gain(u):
                    s = A_SLOT[u]
                    dve.wait_ge(a_tr, i * A_TILES + (u + 1))
                    times_gain(hT[:, :, bass.ts(i * A_TILES + u, P)], ps[:, 1024 * s:1024 * s + 1024]
                               .rearrange("p (k n) -> p k n", n=P), g1_sb[:, :], P).then_inc(a_out, 1)

                norm(0)
                for u in range(1, A_TILES):
                    norm(u)
                    gain(u - 1)
                gain(A_TILES - 1)
            with dve.Fori(0, FG) as g:
                for pair in range(NT // 2):
                    dve.wait_ge(f_chan, g * 5 + (pair + 1))
                    dve.tensor_copy(f_mix[:, 2 * pair:2 * pair + 2, :],
                                    bank(3 + pair % 2).rearrange("p (t n) -> p t n", n=2 * FD))\
                       .then_inc(f_mixed, 1)
                for c, (c0, cn) in enumerate(CHUNKS):
                    dve.wait_ge(f_pos, g * 3 + (c + 1))
                    dve.tensor_scalar(ofT[:, bass.ds(g, 1), c0:c0 + cn],
                                      bank(5 + c, cn).rearrange("p (o n) -> p o n", o=1), 1.0, None, ALU.mult)\
                       .then_inc(f_out, 1)
            c0, cn = CHUNKS[1]
            dve.wait_ge(f_proj, 3 * FG)
            dve.wait_ge(hx_high, 3)
            dve.tensor_tensor(hx_lo[:, :, c0:c0 + cn], hT[:, :, c0:c0 + cn], hx_hi[1][:, :, :].bitcast(F32),
                              ALU.subtract).then_inc(hx1_ready, 1)
            dve.wait_ge(const_ready, CONSTS)
            with dve.Fori(0, HEADS // 2) as hp:
                for j in range(6):
                    n = j // 3
                    c0, cn = CHUNKS[j % 3]
                    dve.wait_ge(h_rinv, hp * 6 + (j + 1))
                    dve.scalar_tensor_tensor(qkvT[:, n, c0:c0 + cn], bank(j % 3, cn), qk_g[:, n:n + 1],
                                             rinv[j % 2][:, 0:cn], ALU.mult, ALU.mult).then_inc(h_qk, 1)
                for c, (c0, cn) in enumerate(CHUNKS):
                    dve.wait_ge(h_vtr, hp * 3 + (c + 1))
                    dve.tensor_copy(v_tok[:, c0 // P:(c0 + cn) // P, :],
                                    bank(3 + c % 2, cn).rearrange("p (t n) -> p t n", n=P)).then_inc(h_v, 1)

                def add_bias(j):
                    _, rows, row, inner = TILES[j // 2]
                    nk, u, b = rows * GRID, j % P_SLOTS, j % 2
                    table = bias_in[:, j % 2, :, :] if inner else bias_all[:, j % 2, row:row + rows, :]
                    dve.wait_ge(s_ready, hp * 20 + (j + 1))
                    if j == 0:
                        dve.wait_ge(b_step, hp * 8 + 8)
                    if j >= P_SLOTS:
                        dve.wait_ge(p_tr, hp * 20 + (j - P_SLOTS + 1))
                    apart(dve, dve_passed)
                    dve.tensor_tensor_reduce(
                        out=p_sb[u][:, 0:nk], in0=ps[:, 2048 + 1024 * b:2048 + 1024 * b + nk],
                        in1=table.rearrange("p r c -> p (r c)"), scale=1.0, scalar=-3.0e38,
                        op0=ALU.add, op1=ALU.max, accum_out=row_max[:, u:u + 1]).then_inc(s_added, 1)
                    dve.wait_ge(s_added, hp * 20 + (j + 1))
                    dve.tensor_scalar(neg_max[:, u:u + 1], row_max[:, u:u + 1], -1.0, None, ALU.mult)\
                       .then_inc(s_max, 1)

                def normalise(j):
                    nk, u = TILES[j // 2][1] * GRID, j % P_SLOTS
                    dve.wait_ge(p_exp, hp * 20 + (j + 1))
                    dve.reciprocal(row_rec[:, u:u + 1], row_sum[:, u:u + 1]).then_inc(p_rec, 1)
                    dve.wait_ge(p_rec, hp * 20 + (j + 1))
                    dve.tensor_scalar(p_sb[u][:, 0:nk], p_sb[u][:, 0:nk], row_rec[:, u:u + 1], None, ALU.mult)\
                       .then_inc(p_ready, 1)

                def attended(t):
                    dve.wait_ge(pv_done, hp * 20 + (2 * t + 2))
                    dve.tensor_scalar(onaT[:, bass.ds(hp, 1), P * t:P * t + P],
                                      bank(t % 2, P).rearrange("p (o n) -> p o n", o=1), 1.0, None, ALU.mult)\
                       .then_inc(o_out, 1)

                add_bias(0)
                add_bias(1)
                for j in range(20):
                    normalise(j)
                    if j >= 3 and j % 2:
                        attended((j - 3) // 2)
                    if j < 18:
                        add_bias(j + 2)
                attended(NT - 1)
            with dve.Fori(0, KT) as m:
                for c, (c0, cn) in enumerate(CHUNKS):
                    dve.wait_ge(m_sig, m * 6 + (c + 1))
                    dve.wait_ge(m_branch, m * 6 + (c + 1))
                    dve.tensor_tensor(mT[:, bass.ds(m, 1), c0:c0 + cn],
                                      sig[0][:, c0:c0 + cn].rearrange("p (o n) -> p o n", o=1),
                                      bank(BRANCH_BANKS[c], cn).rearrange("p (o n) -> p o n", o=1), ALU.mult)\
                       .then_inc(m_mul, 1)
                for c, (c0, cn) in enumerate(CHUNKS):
                    dve.wait_ge(m_sig, m * 6 + (c + 4))
                    dve.wait_ge(m_branch, m * 6 + (c + 4))
                    dve.tensor_tensor(gated[c % 2][:, 0:cn], sig[1][:, c0:c0 + cn], bank(BRANCH_BANKS[3 + c], cn),
                                      ALU.mult).then_inc(m_mul, 1)
                    dve.wait_ge(m_mul, m * 6 + (c + 10))
                    mc = mT[:, bass.ds(m, 1), c0:c0 + cn]
                    dve.tensor_tensor(mc, gated[c % 2][:, 0:cn].rearrange("p (o n) -> p o n", o=1), mc, ALU.add)\
                       .then_inc(m_out, 1)
                dve.wait_ge(m_out, m * 3 + 3)
                apart(dve, dve_passed)

            def token_slice(t, u, free):
                if free is not None:
                    dve.wait_ge(o_mm, free)
                dve.tensor_scalar(m_tok_hi[u][:, :, :], mT[:, :, bass.ts(t, P)], 1.0, None, ALU.mult)\
                   .then_inc(o_high, 1)
                dve.wait_ge(o_high, t + 1)
                dve.tensor_tensor(m_tok_lo[u][:, :, :], mT[:, :, bass.ts(t, P)], m_tok_hi[u][:, :, :].bitcast(F32),
                                  ALU.subtract).then_inc(o_tok, 1)

            def residual(t, u, i, free):
                dve.wait_ge(o_mm, t + 1)
                dve.wait_ge(r_loaded[u], i * 16 + 16)
                if free:
                    dve.wait_ge(x1_stored[u], i * 16)
                    dve.wait_ge(o_xn, t - 1)
                dve.tensor_tensor(x1[u][:, :], ps[:, 1024 * u:1024 * u + 1024], x_res[u][:, :], ALU.add)\
                   .then_inc(o_x1, 1)

            def normed(t, u, i, free):
                dve.wait_ge(o_stat, t * 3 + 3)
                if free:
                    dve.wait_ge(xn_stored[u], i * 16)
                    dve.wait_ge(o_tr, t - 1)
                dve.tensor_scalar(xn[u][:, :], x1[u][:, :], rstd[:, u:u + 1], None, ALU.mult).then_inc(o_xn, 1)

            def gained(t, u):
                dve.wait_ge(o_tr, t + 1)
                times_gain(h2T[u][:, :, :], ps[:, 2048 + 1024 * u:2048 + 1024 * u + 1024]
                           .rearrange("p (k n) -> p k n", n=P), g2_sb[:, :], P).then_inc(o_h2, 1)

            def logits(t, u):
                dve.wait_ge(o_log, t + 1)
                dve.tensor_scalar(logT[:, bass.ts(t, P)], bank(4 + 2 * u, P, slice(0, EXPERTS)), 1.0, None,
                                  ALU.mult)\
                   .then_inc(o_logc, 1)

            dve.wait_ge(m_out, len(CHUNKS) * KT)
            token_slice(0, 0, None)
            token_slice(1, 1, None)
            for n in range(KT):
                dve.wait_ge(wout_high, n + 1)
                dve.tensor_tensor(w_out_lo[:, n, :], w_out_sb[:, n, :],
                                  w_out_hi[:, n, :].bitcast(F32), ALU.subtract)\
                   .then_inc(wout_split, 1)
            residual(0, 0, 0, False)
            token_slice(2, 0, 1)
            normed(0, 0, 0, False)
            residual(1, 1, 0, False)
            token_slice(3, 1, 2)
            normed(1, 1, 0, False)
            gained(0, 0)
            with dve.Fori(0, NT // 2 - 2) as i:
                for u in range(2):
                    t = i * 2 + (u + 2)
                    residual(t, u, i + 1, True)
                    token_slice(t + 2, u, t + 1)
                    logits(t - 2, u)
                    normed(t, u, i + 1, True)
                    gained(t - 1, 1 - u)
            for u in range(2):
                t = NT - 2 + u
                residual(t, u, NT // 2 - 1, True)
                logits(t - 2, u)
                normed(t, u, NT // 2 - 1, True)
                gained(t - 1, 1 - u)
            logits(NT - 2, 0)
            gained(NT - 1, 1)
            logits(NT - 1, 1)

            count = [0]

            def step(instruction):
                count[0] += 1
                instruction.then_inc(r_dve, 1)
                dve.wait_ge(r_dve, count[0])

            def over_experts(a):
                return a.rearrange("p (t o) -> p t o", o=1).broadcast_to([P, NT, EXPERTS])

            dve.wait_ge(r_tr, 1)
            step(dve.tensor_copy(log_tok[:, :, :], bank(0, NT * EXPERTS).rearrange("p (t e) -> p t e", e=EXPERTS)))
            step(dve.reduce_max(r_max[:, :], log_tok[:, :, :], AX.X))
            step(dve.tensor_tensor(log_tok[:, :, :], log_tok[:, :, :], over_experts(r_max[:, :]), ALU.subtract))
            dve.wait_ge(r_exp, 1)
            step(dve.reduce_sum(r_sum[:, :], aff_tok[:, :, :], AX.X))
            step(dve.reciprocal(r_sum[:, :], r_sum[:, :]))
            step(dve.tensor_tensor(aff_tok[:, :, :], aff_tok[:, :, :], over_experts(r_sum[:, :]), ALU.mult))
            dve.wait_ge(r_tr, 2)
            sample = slice(2 * EXPERTS, LISTS * EXPERTS)
            step(dve.memset(aff[sample, S_SAMPLE:HALF], -1.0))
            step(dve.tensor_copy(aff[0:2 * EXPERTS, :], bank(1, HALF, slice(0, 2 * EXPERTS))))
            step(dve.tensor_copy(aff[sample, 0:S_SAMPLE], bank(1, S_SAMPLE, sample)))
            for k in range(0, CAP_P, 8):
                step(dve.max(top_v[:, k:k + 8], aff[:, :]))
                step(dve.max_index(top_i[:, k:k + 8], top_v[:, k:k + 8], aff[:, :]))
                if k + 8 < CAP_P:
                    step(dve.match_replace(aff[:, :], top_v[:, k:k + 8], aff[:, :], -1.0))
            step(dve.tensor_copy(top_f[:, :], top_i[:, :]))
            dve.sem_inc(r_exp, 1)
            dve.wait_ge(r_tr, 3)
            columns = bank(0, 2 * LISTS * EXPERTS).rearrange("p (a n) -> p a n", n=LISTS * EXPERTS)
            dve.tensor_copy(half_2[:, :, :], columns[:, :, EXPERTS:2 * EXPERTS]).then_inc(r_half, 1)
            step(dve.tensor_copy(sought[:, :, :], columns[:, :, 0:EXPERTS]))
            dve.wait_ge(r_tr, 4)
            step(dve.tensor_copy(turned[:, :, :], bank(1, 2 * EXPERTS).rearrange("p (a n) -> p a n", n=EXPERTS)))
            step(dve.tensor_tensor(from_1[:, :], sought[:, 0, :], turned[:, 0, :], ALU.is_ge))
            dve.tensor_tensor(gate_t[:, 0, 0:EXPERTS], sought[:, 0, :], turned[:, 0, :], ALU.max)
            step(dve.tensor_scalar(turned[:, 1, :], turned[:, 1, :], float(HALF), None, ALU.add))
            step(dve.tensor_tensor(sought[:, 1, :], sought[:, 1, :], turned[:, 1, :], ALU.subtract))
            step(dve.tensor_tensor(sought[:, 1, :], sought[:, 1, :], from_1[:, :], ALU.mult))
            step(dve.tensor_tensor(sought[:, 1, :], sought[:, 1, :], turned[:, 1, :], ALU.add))
            dve.tensor_copy(idx_t[:, 0, 0:EXPERTS], sought[:, 1, :])
            s0 = 2 * EXPERTS
            step(dve.tensor_scalar(turned[0:CAP_S, 1, :], bank(0, EXPERTS, slice(0, CAP_S), LISTS * EXPERTS + s0),
                                   float(S_PROMPT), None, ALU.add))
            dve.tensor_copy(gate_t[0:CAP_S, 1, 0:EXPERTS], bank(0, EXPERTS, slice(0, CAP_S), s0))
            dve.tensor_copy(idx_t[0:CAP_S, 1, 0:EXPERTS], turned[0:CAP_S, 1, :]).then_inc(cols_ready, 1)

            def expert_tokens(n):
                dve.wait_ge(x_tr, n + 1)
                for b, k0, kn in X_BANKS:
                    op = times_gain(x_f[:, k0:k0 + kn, :], bank(b, kn * CAP).rearrange("p (k n) -> p k n", n=CAP),
                                    g2_sb[:, k0:k0 + kn], CAP)
                op.then_inc(xf_ready, 1)
                dve.wait_ge(xf_ready, n + 1)
                dve.tensor_copy(x_b[:, :, :], x_f[:, :, :])

            def token_low(n):
                dve.wait_ge(x_hi_ready, n + 1)
                dve.tensor_tensor(x_hl[:, :, 1, :], x_f[:, :, :], x_hl[:, :, 0, :].bitcast(F32), ALU.subtract)\
                   .then_inc(x_ready, 1)

            expert_tokens(0)
            token_low(0)
            with dve.Fori(0, EXPERTS) as e:
                def split(v):
                    if v % UNITS in DVES:
                        low_part(dve, e, v, lo_dve)

                def add_lows(j):
                    dve.wait_ge(low_ready, e * FT + (j + 1))
                    dve.tensor_tensor(gu[j % 2][:, :, :], gate_up(2 * (j % 2))[:, :, 0:CAP], lows[j % 2][:, :, :],
                                      ALU.add).then_inc(gu_added, 1)

                def gated_up(j):
                    dve.wait_ge(silu_ready, e * FT + (j + 1))
                    if j >= 4 and j % 2 == 0:
                        dve.wait_ge(act_hi_ready, e * 8 + (j // 2 - 1))
                    dve.tensor_tensor(act_f[j // 2 % 2][:, j % 2, :], silu[j % 2][:, :], gu[j % 2][:, 1, :],
                                      ALU.mult).then_inc(act_f_ready, 1)

                def act_low(pair):
                    pairs = slice(2 * pair, 2 * pair + 2)
                    dve.wait_ge(act_f_ready, e * FT + (2 * pair + 2))
                    dve.tensor_copy(act_b[:, pairs, :], act_f[pair % 2][:, :, :])
                    dve.wait_ge(act_hi_ready, e * 8 + (pair + 1))
                    dve.tensor_tensor(act_hl[:, pairs, 1, :], act_f[pair % 2][:, :, :],
                                      act_hl[:, pairs, 0, :].bitcast(F32), ALU.subtract).then_inc(act_ready, 1)

                def add_y_lows(d):
                    dve.wait_ge(y_low_ready, e * KT + (d + 1))
                    if d >= 2:
                        dve.wait_ge(y_tr, e * KT + (d - 1))
                    dve.tensor_tensor(yT[d % 2][:, :], bank(4 + d % 2, CAP), y_low[d % 2][:, :], ALU.add)\
                       .then_inc(yT_ready, 1)

                def gated_rows(half):
                    p, q = Y_BANKS[half]
                    cols = slice(BANK * half, BANK * half + BANK)
                    dve.wait_ge(y_tr, e * KT + (4 * half + 4))
                    dve.tensor_scalar(ye_p[:, cols], bank(p), gate_now[:, 0:1], None, ALU.mult).then_inc(y_ready, 1)
                    dve.tensor_scalar(ye_s[:, cols], bank(q, BANK, slice(0, CAP_S)), gate_now[0:CAP_S, 1:2], None,
                                      ALU.mult).then_inc(y_ready, 1)

                for step in range(8):
                    if step:
                        add_lows(2 * step - 1)
                        split(ahead(step)[0])
                        gated_up(2 * step - 1)
                        add_lows(2 * step)
                    else:
                        add_lows(0)
                        split(ahead(0)[0])
                    split(ahead(step)[1])
                    if step:
                        act_low(step - 1)
                    gated_up(2 * step)
                add_lows(FT - 1)
                gated_up(FT - 1)
                act_low(7)
                for d in range(KT):
                    split(ahead(8 + d)[0])
                    if d == 0:
                        expert_tokens(e + 1)
                    add_y_lows(d)
                    if d == 2:
                        token_low(e + 1)
                    if d == 4:
                        dve.wait_ge(cols_ready, e + 2)
                        gated_rows(0)
                gated_rows(1)

        @block.tensor
        def _(pe):
            def product(out, pairs):
                for n, (lhsT, rhs) in enumerate(pairs):
                    op = pe.matmul(out, lhsT, rhs, start=n == 0, stop=n == len(pairs) - 1)
                return op

            pe.sem_inc(m_gate, 6)
            pe.wait_ge(const_ready, CONSTS)
            pe.wait_ge(ident_ready, 2)
            with pe.Fori(0, NT // A_TILES) as i:
                for u in range(A_TILES):
                    s = A_SLOT[u]
                    pe.wait_ge(a_norm, i * A_TILES + (u + 1))
                    for k in range(KT):
                        op = pe.transpose(ps[:, 1024 * s + P * k:1024 * s + P * k + P],
                                          xn_a[s][:, P * k:P * k + P], ident[:, :])
                    op.then_inc(a_tr, 1)
            pe.wait_ge(a_out, NT)
            with pe.Fori(0, FG) as g:
                pe.wait_ge(f_loaded, g * 16 + 16)
                for c, (c0, cn) in enumerate(CHUNKS):
                    op = product(bank(c, cn), [(f_w[:, k, :], hT[:, k, c0:c0 + cn]) for k in range(KT)])
                    op.then_inc(f_proj, 1)
                pe.wait_ge(dft_loaded, 16)
                for pair in range(NT // 2):
                    pe.wait_ge(f_copied, g * 3 + (pair // 2 + 1))
                    if pair >= 2:
                        pe.wait_ge(f_mixed, g * 5 + (pair - 1))
                    for t in (2 * pair, 2 * pair + 1):
                        op = pe.matmul(bank(3 + pair % 2, 2 * FD, first=2 * FD * (t % 2)),
                                       fT[:, P * t:P * t + P], dft_sb[:, :], start=True, stop=True)
                    op.then_inc(f_chan, 1)
                pe.wait_ge(f_mixed, g * 5 + 5)
                pe.wait_ge(f_tables, 16 * 4)
                for c, (c0, cn) in enumerate(CHUNKS):
                    prompt = c0 < S_PROMPT
                    tiles = range(PT_TILES) if prompt else range(PT_TILES, NT)
                    pairs = []
                    for t in tiles:
                        for half, table in enumerate((pos_c_sb, pos_s_sb) if prompt else (spos_c_sb, spos_s_sb)):
                            rhs = table[:, t, c0:c0 + cn] if prompt else table[:, t - PT_TILES, :]
                            pairs.append((f_mix[:, t, FD * half:FD * half + FD], rhs))
                    product(bank(5 + c, cn), pairs).then_inc(f_pos, 1)
            def wait_tokens(c):
                if c == 1:
                    pe.wait_ge(hx1_ready, 1)
                else:
                    pe.wait_ge(hx_ready, c // 2 + 1)

            def three_passes(b, c, n):
                c0, cn = CHUNKS[c]
                high, low = hx_hi[c][:, :, :], hx_lo[:, :, c0:c0 + cn]
                return product(bank(b, cn), [(w_high[n][:, k, :], high[:, k, :]) for k in range(KT)]
                               + [(w_high[n][:, k, :], low[:, k, :]) for k in range(KT)]
                               + [(w_low[n][:, k, :], high[:, k, :]) for k in range(KT)])

            pe.wait_ge(f_out, 3 * FG)
            with pe.Fori(0, HEADS // 2) as hp:
                def sum_squares(j):
                    cn = CHUNKS[j % 3][1]
                    pe.wait_ge(h_sq, hp * 6 + (j + 1))
                    if j >= 2:
                        pe.wait_ge(h_ln, hp * 6 + (j - 1))
                    pe.matmul(bank(3 + j % 2, cn), head_ones[:, :], sq[j % 2][:, 0:cn], start=True, stop=True)\
                      .then_inc(h_ss, 1)

                def values(c):
                    c0, cn = CHUNKS[c]
                    pe.wait_ge(h_vT, hp * 3 + (c + 1))
                    if c == 0:
                        pe.wait_ge(h_ln, hp * 6 + 6)
                    if c == 2:
                        pe.wait_ge(h_v, hp * 3 + 1)
                    for t in range(cn // P):
                        op = pe.transpose(bank(3 + c % 2, P, first=P * t), qkvT[:, 2, c0 + P * t:c0 + P * t + P],
                                          ident[:, :])
                    op.then_inc(h_vtr, 1)

                pe.wait_ge(o_out, hp * NT + 1)
                for j in range(9):
                    c0, cn = CHUNKS[j % 3]
                    if j >= 3:
                        pe.wait_ge(h_qk, hp * 6 + (j - 2))
                    if j < 3:
                        wait_tokens(c=j)
                    if j % 3 == 0:
                        pe.wait_ge(h_split, hp * 3 + (j // 3 + 1))
                    three_passes(j % 3, j % 3, j // 3).then_inc(h_proj, 1)
                    if 1 <= j < 7:
                        sum_squares(j - 1)
                    if j >= 7:
                        values(j - 7)
                values(2)

                def scores(j):
                    t, hh = j // 2, j % 2
                    key0, rows, _, _ = TILES[t]
                    part = slice(DH * hh, DH * hh + DH)
                    at0 = 2048 + 1024 * (j % 2)
                    if j >= 2:
                        pe.wait_ge(s_added, hp * 20 + (j - 1))
                    n = min(rows * GRID, BANK)
                    op = pe.matmul(ps[:, at0:at0 + n], qkvT[part, 0, P * t:P * t + P],
                                   qkvT[part, 1, key0:key0 + n], start=True, stop=True)
                    if rows > KH:
                        op = pe.matmul(ps[:, at0 + n:at0 + n + P], qkvT[part, 0, P * t:P * t + P],
                                       qkvT[part, 1, key0 + n:key0 + n + P], start=True, stop=True)
                    op.then_inc(s_ready, 1)

                def transposed(j):
                    nk = TILES[j // 2][1] * GRID
                    pe.wait_ge(p_ready, hp * 20 + (j + 1))
                    if j >= 1:
                        pe.wait_ge(p_copied, hp * 20 + j)
                    for k in range(min(nk // P, 4)):
                        op = pe.transpose(bank(2, P, first=P * k), p_sb[j % P_SLOTS][:, P * k:P * k + P], ident[:, :])
                    if nk > 4 * P:
                        op = pe.transpose(bank(3, P, slice(0, GRID)), p_sb[j % P_SLOTS][:, 4 * P:nk], ident[:, :])
                    op.then_inc(p_tr, 1)

                def attend(j):
                    t, hh = j // 2, j % 2
                    key0, rows, _, _ = TILES[t]
                    first, nk = key0 // P, rows * GRID
                    cols = slice(DH * hh, DH * hh + DH)
                    pe.wait_ge(p_copied, hp * 20 + (j + 1))
                    if t >= 2:
                        pe.wait_ge(o_out, hp * NT + t)
                    pairs = [(v_tok[:, first + k, cols], pT[j % 2][:, k, :]) for k in range(min(nk // P, 4))]
                    if nk > 4 * P:
                        pairs.append((v_tok[0:GRID, first + 4, cols], pT[j % 2][0:GRID, 4, :]))
                    product(bank(t % 2, P, cols), pairs).then_inc(pv_done, 1)

                pe.wait_ge(h_qk, hp * 6 + 6)
                pe.wait_ge(h_v, hp * 3 + 3)
                scores(0)
                scores(1)
                for j in range(20):
                    if j < 18:
                        scores(j + 2)
                    transposed(j)
                    if j >= 1:
                        attend(j - 1)
                attend(19)
            pe.wait_ge(o_out, HEADS // 2 * NT + 1)
            with pe.Fori(0, KT) as m:
                for q in range(6):
                    u, c = q // 3, q % 3
                    c0, cn = CHUNKS[c]
                    if c == 0:
                        pe.wait_ge(m_split, m * 2 + (u + 1))
                    if q < 4:
                        pe.wait_ge(m_mul, m * 6 + (q + 3))
                    three_passes(q, c, u).then_inc(m_gate, 1)
                for q in range(6):
                    u, c = q // 3, q % 3
                    c0, cn = CHUNKS[c]
                    if c == 0:
                        pe.wait_ge(m_w_loaded[u], m * 16 + 16)
                    if q >= 2:
                        pe.wait_ge(m_sig, m * 6 + (q - 1))
                    product(bank(BRANCH_BANKS[q], cn),
                            [(m_w[u][:, k, :], (onaT, ofT)[u][:, k, c0:c0 + cn]) for k in range(4)])\
                        .then_inc(m_branch, 1)

            def project(t, u, free, arriving=False):
                pe.wait_ge(o_tok, t + 1)
                if free is not None:
                    pe.wait_ge(o_x1, free)
                for k in range(KT):
                    if arriving:
                        pe.wait_ge(wout_split, k + 1)
                    passes = ((m_tok_hi, w_out_hi), (m_tok_hi, w_out_lo), (m_tok_lo, w_out_hi))
                    for n, (tokens, weights) in enumerate(passes):
                        for half in range(2):
                            op = pe.matmul(bank(2 * u + half), tokens[u][:, k, :],
                                           weights[:, k, BANK * half:BANK * half + BANK],
                                           start=k == 0 and n == 0, stop=k == KT - 1 and n == 2)
                op.then_inc(o_mm, 1)

            def turn(t, u, free):
                pe.wait_ge(o_xn, t + 1)
                if free is not None:
                    pe.wait_ge(o_logc, free)
                for k in range(KT):
                    op = pe.transpose(ps[:, 2048 + 1024 * u + P * k:2048 + 1024 * u + P * k + P],
                                      xn[u][:, P * k:P * k + P], ident[:, :])
                op.then_inc(o_tr, 1)

            def route(t, u):
                pe.wait_ge(o_h2, t + 1)
                product(bank(4 + 2 * u, P, slice(0, EXPERTS)),
                        [(wr_sb[:, k, :], h2T[u][:, k, :]) for k in range(KT)]).then_inc(o_log, 1)

            pe.wait_ge(m_out, len(CHUNKS) * KT)
            project(0, 0, None, arriving=True)
            project(1, 1, None)
            turn(0, 0, None)
            project(2, 0, 1)
            route(0, 0)
            turn(1, 1, None)
            with pe.Fori(0, NT // 2 - 2) as i:
                project(i * 2 + 3, 1, i * 2 + 2)
                route(i * 2 + 1, 1)
                turn(i * 2 + 2, 0, i * 2 + 1)
                project(i * 2 + 4, 0, i * 2 + 3)
                route(i * 2 + 2, 0)
                turn(i * 2 + 3, 1, i * 2 + 2)
            project(NT - 1, 1, NT - 2)
            route(NT - 3, 1)
            turn(NT - 2, 0, NT - 3)
            route(NT - 2, 0)
            turn(NT - 1, 1, NT - 2)
            route(NT - 1, 1)

            pe.wait_ge(o_logc, NT)
            for n, t in enumerate(LIST_TILES):
                op = pe.transpose(bank(0, EXPERTS, first=EXPERTS * n), logT[:, P * t:P * t + P],
                                  ident[0:EXPERTS, 0:EXPERTS])
            op.then_inc(r_tr, 1)
            pe.wait_ge(r_dve, 6)
            for t in range(HALF // P):
                lists, first = len(range(t, NT, HALF // P)), LIST_TILES.index(t)
                op = pe.transpose(bank(1, P, slice(0, lists * EXPERTS), P * t),
                                  aff_tok[:, first:first + lists, :].rearrange("p a e -> p (a e)"), ident[:, :])
            op.then_inc(r_tr, 1)
            pe.wait_ge(r_exp, 2)
            for n, src in enumerate((top_v, top_f)):
                op = pe.transpose(bank(0, LISTS * EXPERTS, first=LISTS * EXPERTS * n), src[:, :],
                                  ident[0:LISTS * EXPERTS, 0:LISTS * EXPERTS])
            op.then_inc(r_tr, 1)
            pe.wait_ge(r_half, 1)
            pe.wait_ge(anti_ready, 2)
            pe.matmul(bank(1, 2 * EXPERTS), anti[:, :], half_2[:, :, :].rearrange("p a n -> p (a n)"),
                      start=True, stop=True).then_inc(r_tr, 1)

            def expert_transposes():
                for b, k0, kn in X_BANKS:
                    for k in range(k0, k0 + kn):
                        col = CAP * (k - k0)
                        pe.transpose(bank(b, P, first=col), xg_p[:, P * k:P * k + P], ident[:, :])
                        op = pe.transpose(bank(b, CAP_S, first=col + P), xg_s[:, P * k:P * k + P],
                                          ident[0:CAP_S, 0:CAP_S])
                op.then_inc(x_tr, 1)

            def split_product(out, n, v, cols, hl, b, part=None):
                part = part or range(n)
                for k in part:
                    pe.matmul(out, unit(w_hi, v)[:, k, cols], hl[:, k, :, :].rearrange("p a n -> p (a n)"),
                              start=k == 0, stop=False)
                for k in part:
                    op = pe.matmul(out[:, CAP:2 * CAP], unit(w_lo, v)[:, k, cols], b[:, k, :],
                                   start=False, stop=k == n - 1)
                return op

            def tile_of_gate_and_up(e, j):
                b = 2 * (j % 2)
                for n in range(2):
                    v = j // 2 * 2 + n
                    if j % 2 == 0:
                        wait_split(pe, e, v)
                    op = split_product(bank(b + n, 2 * CAP), KT, v, slice(P * (j % 2), P * (j % 2) + P), x_hl, x_b)
                op.then_inc(gu_ready, 1)

            pe.sem_inc(down_ready, KT)
            pe.wait_ge(rows_moved, 32)
            expert_transposes()
            pe.wait_ge(first_units, LEAD)
            pe.wait_ge(x_ready, 1)
            tile_of_gate_and_up(0, 0)
            with pe.Fori(0, EXPERTS) as e:
                for j in range(1, FT):
                    if j >= 2:
                        pe.wait_ge(gu_added, e * FT + (j - 1))
                    tile_of_gate_and_up(e, j)
                pe.wait_ge(gu_added, e * FT + (FT - 1))
                pe.wait_ge(y_ready, e * 4 + 1)
                pe.wait_ge(rows_moved, e * 64 + 64)
                expert_transposes()

                def back(d):
                    (p, q), col = Y_BANKS[d // 4], P * (d % 4)
                    pe.wait_ge(yT_ready, e * KT + (d + 1))
                    if d == 4:
                        pe.wait_ge(xf_ready, e + 2)
                    pe.transpose(bank(p, P, first=col), yT[d % 2][:, 0:P], ident[:, :])
                    pe.transpose(bank(q, P, slice(0, CAP_S), col), yT[d % 2][:, P:CAP], ident[:, :])\
                      .then_inc(y_tr, 1)

                for d in range(KT):
                    wait_split(pe, e, 16 + d)
                    if d >= 2:
                        pe.wait_ge(yT_ready, e * KT + (d - 1))
                    out = bank(4 + d % 2, 2 * CAP)
                    if d == 0:
                        for k0, k1 in ((0, FT - 4), (FT - 4, FT - 2), (FT - 2, FT)):
                            pe.wait_ge(act_ready, e * 8 + k1 // 2)
                            op = split_product(out, FT, 16, slice(0, P), act_hl, act_b, range(k0, k1))
                    else:
                        op = split_product(out, FT, 16 + d, slice(0, P), act_hl, act_b)
                    op.then_inc(down_ready, 1)
                    if d >= 1:
                        back(d - 1)
                pe.wait_ge(x_ready, e + 2)
                pe.wait_ge(y_ready, e * 4 + 3)
                tile_of_gate_and_up(e + 1, 0)
                back(KT - 1)


def dft_tables():
    def angles(n):
        return 2.0 * np.pi * (np.outer(np.arange(n), np.arange(n)) % n) / n

    a = angles(FD)
    tables = [np.concatenate([np.cos(a), np.sin(a)], 1)]
    for n in (S_PROMPT, S_SAMPLE):
        norm = 1.0 / np.sqrt(n * FD)
        tables += [np.cos(angles(n)) * norm, -np.sin(angles(n)) * norm]
    return [t.astype(np.float32) for t in tables]


def window_mask():
    c = np.arange(GRID)[:, None]
    c0 = np.clip(c - KW // 2, 0, GRID - KW)
    k = np.arange(GRID)[None, :]
    one = np.where((k >= c0) & (k < c0 + KW), 0.0, MASKED).astype(np.float32)
    return np.concatenate([one, one], 0)


def kernel(x_prompt, x_sample, norm1_g, w_in, q_norm_g, k_norm_g, rpb, w_na_out, w_fourier, w_out,
           norm2_g, w_router, w_gate_e, w_up_e, w_down_e):
    import concourse.bacc as bacc
    from concourse.bass_utils import run_bass_kernel_spmd

    arrays = {"x": np.concatenate([np.asarray(x_prompt)[0], np.asarray(x_sample)[0]], 0)}
    for name, a in (("g1", norm1_g), ("w_in", w_in), ("q_g", q_norm_g), ("k_g", k_norm_g), ("rpb", rpb),
                    ("w_na", w_na_out), ("w_fo", w_fourier), ("w_out", w_out), ("g2", norm2_g),
                    ("w_r", w_router), ("w_g", w_gate_e), ("w_u", w_up_e), ("w_d", w_down_e)):
        arrays[name] = np.ascontiguousarray(np.asarray(a)[0])
    for name in ("g1", "g2"):
        arrays[name] = np.ascontiguousarray(arrays[name].reshape(KT, P).T)
    for name, a in zip(("dft_c", "pos_c", "pos_s", "spos_c", "spos_s"), dft_tables()):
        arrays[name] = a
    arrays["col_mask"] = window_mask()
    nc = bacc.Bacc("TRN2", target_bir_lowering=False, num_devices=1)
    arrays = {f"in_{k}": v for k, v in arrays.items()}
    args = [nc.dram_tensor(k, v.shape, mybir.dt.from_np(v.dtype), kind="ExternalInput").ap()
            for k, v in arrays.items()]
    y = nc.dram_tensor("y_out", (TOK, D), F32, kind="ExternalOutput").ap()
    build(nc, *args, y)
    r = run_bass_kernel_spmd(nc, [arrays], core_ids=[0])
    got = r.results[0]["y_out"]
    return got[None, :S_PROMPT], got[None, S_PROMPT:]
```
